# Optimizing a Trainium2 kernel written in Bass

```python
import math
import jax
import jax.numpy as jnp
from jax import lax
import numpy as np

D_MODEL = 1024
BATCH = 1
SEQ = 256
DEPTH = 1
DEC_BATCH = 1
DEC_SEQ = 32
PAST_LEN = 256

CHUNK = 64
HEAD_DIM = 64
ATTN_SCALE = HEAD_DIM ** -0.5
A_HEADS = 4
A_WIDTH = A_HEADS * HEAD_DIM
A_PREV_CHUNKS = 8
A_REACH = A_PREV_CHUNKS * CHUNK
A_REL_CLIP = 128
B_HEADS = 8
B_KV_HEADS = 2
B_GROUP = B_HEADS // B_KV_HEADS
B_WIDTH = B_HEADS * HEAD_DIM
B_KV_WIDTH = B_KV_HEADS * HEAD_DIM
B_WINDOW = 128
B_PREV_CHUNKS = B_WINDOW // CHUNK
T5_BUCKETS = 32
T5_MAX_DISTANCE = 128
C_CH = D_MODEL // 4
CONV_W = 31
MIX_WIDTH = A_WIDTH + B_WIDTH + C_CH
IN_PROJ_WIDTH = 3 * A_WIDTH + B_WIDTH + 2 * B_KV_WIDTH + 2 * C_CH
SPLIT_POINTS = (A_WIDTH, 2 * A_WIDTH, 3 * A_WIDTH, 3 * A_WIDTH + B_WIDTH,
                3 * A_WIDTH + B_WIDTH + B_KV_WIDTH, 3 * A_WIDTH + B_WIDTH + 2 * B_KV_WIDTH)
N_EXPERTS = 32
TOP_K = 4
D_FF = D_MODEL
SWIGLU_LIMIT = 7.0
SWIGLU_ALPHA = 1.702
EXPERT_BLOCK = 128
DEEPNORM_ALPHA = (2 * DEPTH) ** 0.25
DEEPNORM_BETA = (8 * DEPTH) ** -0.25
LN_EPS = 1e-5
NEG_INF = -1e30

kernel_name = 'hybrid_streaming_encoder_step'

def layer_norm(x, g, b):
    xf = x.astype(jnp.float32)
    mu = jnp.mean(xf, axis=-1, keepdims=True)
    var = jnp.mean(jnp.square(xf - mu), axis=-1, keepdims=True)
    y = (xf - mu) * lax.rsqrt(var + LN_EPS) * g.astype(jnp.float32) + b.astype(jnp.float32)
    return y.astype(x.dtype)

def chunk_band(x, n_prev):
    b, t = x.shape[:2]
    nc = t // CHUNK
    xc = x.reshape(b, nc, CHUNK, *x.shape[2:])
    xp = jnp.concatenate([jnp.zeros((b, n_prev, CHUNK) + x.shape[2:], x.dtype), xc], axis=1)
    idx = np.arange(nc)[:, None] + np.arange(n_prev + 1)[None, :]
    return xp[:, idx].reshape(b, nc, (n_prev + 1) * CHUNK, *x.shape[2:])

def band_valid(nc, n_prev):
    return (np.arange(nc)[:, None] - n_prev + np.arange((n_prev + 1) * CHUNK)[None, :] // CHUNK) >= 0

def band_rel(n_prev):
    return np.arange((n_prev + 1) * CHUNK)[None, :] - n_prev * CHUNK - np.arange(CHUNK)[:, None]

def cache_rel(n_cache, s):
    return np.concatenate([np.arange(n_cache) - n_cache, np.arange(s)])[None, :] - np.arange(s)[:, None]

def clipped_rel_bias(rel, table):
    idx = np.clip(rel, -A_REL_CLIP, A_REL_CLIP) + A_REL_CLIP
    return jnp.moveaxis(table[idx].astype(jnp.float32), -1, 0)

def t5_bucket(rel):
    nb = T5_BUCKETS // 2
    max_exact = nb // 2
    n = np.abs(rel)
    nf = np.maximum(n, 1).astype(np.float32)
    large = max_exact + (np.log(nf / max_exact) / math.log(T5_MAX_DISTANCE / max_exact)
                         * (nb - max_exact)).astype(np.int32)
    large = np.minimum(large, nb - 1)
    return np.where(rel > 0, nb, 0) + np.where(n < max_exact, n, large)

def t5_rel_bias(rel, table):
    return jnp.moveaxis(table[t5_bucket(rel)].astype(jnp.float32), -1, 0)

def sink_softmax(logits, sink):
    m = jnp.maximum(jnp.max(logits, axis=-1, keepdims=True), sink)
    e = jnp.exp(logits - m)
    return e / (jnp.sum(e, axis=-1, keepdims=True) + jnp.exp(sink - m))

def glu(g):
    a, gate = jnp.split(g, 2, axis=-1)
    return a * jax.nn.sigmoid(gate)

def project_heads(h, w_in):
    b, t = h.shape[:2]
    qa, ka, va, qb, kb, vb, g = jnp.split(h @ w_in, list(SPLIT_POINTS), axis=-1)
    heads = lambda a, n: a.reshape(b, t, n, HEAD_DIM)
    return (heads(qa, A_HEADS), heads(ka, A_HEADS), heads(va, A_HEADS),
            heads(qb, B_HEADS), heads(kb, B_KV_HEADS), heads(vb, B_KV_HEADS), glu(g))

def band_attention_a_prompt(q, k, v, table):
    b, t = q.shape[:2]
    nc = t // CHUNK
    qc = q.reshape(b, nc, CHUNK, A_HEADS, HEAD_DIM)
    kb, vb = chunk_band(k, A_PREV_CHUNKS), chunk_band(v, A_PREV_CHUNKS)
    logits = jnp.einsum('bcqhd,bckhd->bhcqk', qc, kb).astype(jnp.float32) * ATTN_SCALE
    logits = logits + clipped_rel_bias(band_rel(A_PREV_CHUNKS), table)[None, :, None]
    logits = jnp.where(band_valid(nc, A_PREV_CHUNKS)[None, None, :, None, :], logits, NEG_INF)
    p = jax.nn.softmax(logits, axis=-1).astype(v.dtype)
    return jnp.einsum('bhcqk,bckhd->bcqhd', p, vb).reshape(b, t, A_WIDTH)

def band_attention_a_sample(q, k_all, v_all, n_cache, table):
    b, s = q.shape[:2]
    logits = jnp.einsum('bqhd,bkhd->bhqk', q, k_all).astype(jnp.float32) * ATTN_SCALE
    logits = logits + clipped_rel_bias(cache_rel(n_cache, s), table)[None]
    p = jax.nn.softmax(logits, axis=-1).astype(v_all.dtype)
    return jnp.einsum('bhqk,bkhd->bqhd', p, v_all).reshape(b, s, A_WIDTH)

def window_attention_b_prompt(q, k, v, table, sinks):
    b, t = q.shape[:2]
    nc = t // CHUNK
    qc = q.reshape(b, nc, CHUNK, B_KV_HEADS, B_GROUP, HEAD_DIM)
    kb, vb = chunk_band(k, B_PREV_CHUNKS), chunk_band(v, B_PREV_CHUNKS)
    logits = jnp.einsum('bcqngd,bcknd->bngcqk', qc, kb).astype(jnp.float32) * ATTN_SCALE
    bias = t5_rel_bias(band_rel(B_PREV_CHUNKS), table).reshape(B_KV_HEADS, B_GROUP, CHUNK, -1)
    logits = logits + bias[None, :, :, None]
    logits = jnp.where(band_valid(nc, B_PREV_CHUNKS)[None, None, None, :, None, :], logits, NEG_INF)
    sink = sinks.astype(jnp.float32).reshape(B_KV_HEADS, B_GROUP)[None, :, :, None, None, None]
    p = sink_softmax(logits, sink).astype(v.dtype)
    return jnp.einsum('bngcqk,bcknd->bcqngd', p, vb).reshape(b, t, B_WIDTH)

def window_attention_b_sample(q, k_all, v_all, n_cache, table, sinks):
    b, s = q.shape[:2]
    qg = q.reshape(b, s, B_KV_HEADS, B_GROUP, HEAD_DIM)
    logits = jnp.einsum('bqngd,bknd->bngqk', qg, k_all).astype(jnp.float32) * ATTN_SCALE
    bias = t5_rel_bias(cache_rel(n_cache, s), table).reshape(B_KV_HEADS, B_GROUP, s, -1)
    logits = logits + bias[None]
    sink = sinks.astype(jnp.float32).reshape(B_KV_HEADS, B_GROUP)[None, :, :, None, None]
    p = sink_softmax(logits, sink).astype(v_all.dtype)
    return jnp.einsum('bngqk,bknd->bqngd', p, v_all).reshape(b, s, B_WIDTH)

def conv_module_tail(u_ext, conv_w, conv_b, ln_g, ln_b):
    y = lax.conv_general_dilated(u_ext, conv_w[:, None, :].astype(u_ext.dtype), window_strides=(1,),
                                 padding='VALID', dimension_numbers=('NWC', 'WIO', 'NWC'),
                                 feature_group_count=C_CH)
    return jax.nn.silu(layer_norm(y + conv_b, ln_g, ln_b))

def mixer_prompt(h, w_in, w_out, rel_a, t5_table, sinks, conv_w, conv_b, cln_g, cln_b):
    b, t = h.shape[:2]
    qa, ka, va, qb, kb, vb, u = project_heads(h, w_in)
    oa = band_attention_a_prompt(qa, ka, va, rel_a)
    ob = window_attention_b_prompt(qb, kb, vb, t5_table, sinks)
    u_ext = jnp.concatenate([jnp.zeros((b, CONV_W - 1, C_CH), u.dtype), u], axis=1)
    oc = conv_module_tail(u_ext, conv_w, conv_b, cln_g, cln_b)
    out = jnp.concatenate([oa, ob, oc], axis=-1) @ w_out
    na, nb = min(A_REACH, t), min(B_WINDOW, t)
    state = (ka[:, t - na:], va[:, t - na:], kb[:, t - nb:], vb[:, t - nb:], u_ext[:, -(CONV_W - 1):])
    return out, state

def mixer_sample(h, ca_k, ca_v, cb_k, cb_v, conv_state,
                 w_in, w_out, rel_a, t5_table, sinks, conv_w, conv_b, cln_g, cln_b):
    qa, ka, va, qb, kb, vb, u = project_heads(h, w_in)
    na, nb = ca_k.shape[1], cb_k.shape[1]
    ka_all = jnp.concatenate([ca_k, ka], axis=1)
    va_all = jnp.concatenate([ca_v, va], axis=1)
    kb_all = jnp.concatenate([cb_k, kb], axis=1)
    vb_all = jnp.concatenate([cb_v, vb], axis=1)
    oa = band_attention_a_sample(qa, ka_all, va_all, na, rel_a)
    ob = window_attention_b_sample(qb, kb_all, vb_all, nb, t5_table, sinks)
    u_ext = jnp.concatenate([conv_state, u], axis=1)
    oc = conv_module_tail(u_ext, conv_w, conv_b, cln_g, cln_b)
    out = jnp.concatenate([oa, ob, oc], axis=-1) @ w_out
    state = (ka_all[:, -na:], va_all[:, -na:], kb_all[:, -nb:], vb_all[:, -nb:], u_ext[:, -(CONV_W - 1):])
    return out, state

def moe_ffn(h, w_router, b_router, w_e_in, b_e_in, w_e_out, b_e_out):
    b, t, d = h.shape
    n_tok = b * t
    n_assign = n_tok * TOP_K
    tok = h.reshape(n_tok, d)
    logits = (tok @ w_router).astype(jnp.float32) + b_router.astype(jnp.float32)
    top_val, top_idx = lax.top_k(logits, TOP_K)
    gate = jax.nn.softmax(top_val, axis=-1)
    flat_e = top_idx.reshape(n_assign)
    order = jnp.argsort(flat_e)
    sorted_e = flat_e[order]
    counts = jnp.bincount(flat_e, length=N_EXPERTS)
    padded = (counts + EXPERT_BLOCK - 1) // EXPERT_BLOCK * EXPERT_BLOCK
    pad_end = jnp.cumsum(padded)
    pad_start = pad_end - padded
    grp_start = jnp.cumsum(counts) - counts
    slot_sorted = pad_start[sorted_e] + jnp.arange(n_assign) - grp_start[sorted_e]
    slot = jnp.zeros((n_assign,), jnp.int32).at[order].set(slot_sorted.astype(jnp.int32))
    n_blocks = -(-n_assign // EXPERT_BLOCK) + N_EXPERTS
    rows = jnp.zeros((n_blocks * EXPERT_BLOCK, d), tok.dtype).at[slot].set(jnp.repeat(tok, TOP_K, axis=0))
    block_e = jnp.minimum(jnp.searchsorted(pad_end, jnp.arange(n_blocks) * EXPERT_BLOCK, side='right'),
                          N_EXPERTS - 1)

    def expert_block(args):
        xb, e = args
        hid = xb @ w_e_in[e] + b_e_in[e]
        x_glu, x_lin = jnp.split(hid, 2, axis=-1)
        x_glu = jnp.minimum(x_glu, SWIGLU_LIMIT)
        x_lin = jnp.clip(x_lin, -SWIGLU_LIMIT, SWIGLU_LIMIT)
        act = x_glu * jax.nn.sigmoid(SWIGLU_ALPHA * x_glu) * (x_lin + 1.0)
        return act @ w_e_out[e] + b_e_out[e]

    out_rows = lax.map(expert_block, (rows.reshape(n_blocks, EXPERT_BLOCK, d), block_e))
    picked = out_rows.reshape(n_blocks * EXPERT_BLOCK, d)[slot].reshape(n_tok, TOP_K, d)
    y = jnp.einsum('nk,nkd->nd', gate.astype(picked.dtype), picked)
    return y.reshape(b, t, d)

def trunk_layer(x, c, mixer, w_ada, b_ada, ln_g, ln_b, w_router, b_router, w_e_in, b_e_in, w_e_out, b_e_out):
    mod = jax.nn.silu(c) @ w_ada + b_ada
    sh1, sc1, g1, sh2, sc2, g2 = jnp.split(mod[:, None, :], 6, axis=-1)
    mix, state = mixer(x * (1.0 + sc1) + sh1)
    x = layer_norm(DEEPNORM_ALPHA * x + g1 * mix, ln_g[0], ln_b[0])
    ffn = moe_ffn(x * (1.0 + sc2) + sh2, w_router, b_router, w_e_in, b_e_in, w_e_out, b_e_out)
    x = layer_norm(DEEPNORM_ALPHA * x + g2 * ffn, ln_g[1], ln_b[1])
    return x, state

def setup_inputs(seed: int = 0) -> dict:
    key = jax.random.key(seed)
    ks = jax.random.split(key, 32)
    f32 = jnp.float32

    def normal(k, shape, scale):
        return jax.random.normal(k, shape, f32) * scale

    a_cache = min(A_REACH, PAST_LEN)
    b_cache = min(B_WINDOW, PAST_LEN)
    return {
        'x_prompt': normal(ks[0], (BATCH, SEQ, D_MODEL), 1.0),
        'x_sample': normal(ks[1], (DEC_BATCH, DEC_SEQ, D_MODEL), 1.0),
        'cache_a_k': normal(ks[2], (DEPTH, DEC_BATCH, a_cache, A_HEADS, HEAD_DIM), 1.0),
        'cache_a_v': normal(ks[3], (DEPTH, DEC_BATCH, a_cache, A_HEADS, HEAD_DIM), 1.0),
        'cache_b_k': normal(ks[4], (DEPTH, DEC_BATCH, b_cache, B_KV_HEADS, HEAD_DIM), 1.0),
        'cache_b_v': normal(ks[5], (DEPTH, DEC_BATCH, b_cache, B_KV_HEADS, HEAD_DIM), 1.0),
        'state_conv': normal(ks[6], (DEPTH, DEC_BATCH, CONV_W - 1, C_CH), 0.5),
        'c_prompt': normal(ks[7], (BATCH, D_MODEL), 1.0),
        'c_sample': normal(ks[8], (DEC_BATCH, D_MODEL), 1.0),
        'w_in': normal(ks[9], (DEPTH, D_MODEL, IN_PROJ_WIDTH), D_MODEL ** -0.5),
        'w_out': normal(ks[10], (DEPTH, MIX_WIDTH, D_MODEL), MIX_WIDTH ** -0.5 * DEEPNORM_BETA),
        'rel_bias_a': normal(ks[11], (DEPTH, 2 * A_REL_CLIP + 1, A_HEADS), 0.1),
        't5_bias': normal(ks[12], (T5_BUCKETS, B_HEADS), 0.1),
        'sinks': normal(ks[13], (DEPTH, B_HEADS), 0.5),
        'conv_w': normal(ks[14], (DEPTH, CONV_W, C_CH), CONV_W ** -0.5),
        'conv_b': normal(ks[15], (DEPTH, C_CH), 0.02),
        'conv_ln_g': 1.0 + normal(ks[16], (DEPTH, C_CH), 0.05),
        'conv_ln_b': normal(ks[17], (DEPTH, C_CH), 0.02),
        'w_ada': normal(ks[18], (DEPTH, D_MODEL, 6 * D_MODEL), 0.5 * D_MODEL ** -0.5),
        'b_ada': normal(ks[19], (DEPTH, 6 * D_MODEL), 0.02),
        'ln_g': 1.0 + normal(ks[20], (DEPTH, 2, D_MODEL), 0.05),
        'ln_b': normal(ks[21], (DEPTH, 2, D_MODEL), 0.02),
        'w_router': normal(ks[22], (DEPTH, D_MODEL, N_EXPERTS), D_MODEL ** -0.5),
        'b_router': normal(ks[23], (DEPTH, N_EXPERTS), 0.01),
        'w_e_in': normal(ks[24], (DEPTH, N_EXPERTS, D_MODEL, 2 * D_FF), D_MODEL ** -0.5),
        'b_e_in': normal(ks[25], (DEPTH, N_EXPERTS, 2 * D_FF), 0.02),
        'w_e_out': normal(ks[26], (DEPTH, N_EXPERTS, D_FF, D_MODEL), D_FF ** -0.5 * DEEPNORM_BETA),
        'b_e_out': normal(ks[27], (DEPTH, N_EXPERTS, D_MODEL), 0.02),
    }

def reference(x_prompt, x_sample, cache_a_k, cache_a_v, cache_b_k, cache_b_v, state_conv,
              c_prompt, c_sample, w_in, w_out, rel_bias_a, t5_bias, sinks, conv_w, conv_b,
              conv_ln_g, conv_ln_b, w_ada, b_ada, ln_g, ln_b, w_router, b_router,
              w_e_in, b_e_in, w_e_out, b_e_out):
    xp, xs = x_prompt, x_sample
    states_p, states_s = [], []
    for l in range(DEPTH):
        mix_w = (w_in[l], w_out[l], rel_bias_a[l], t5_bias, sinks[l],
                 conv_w[l], conv_b[l], conv_ln_g[l], conv_ln_b[l])
        ffn_w = (w_ada[l], b_ada[l], ln_g[l], ln_b[l], w_router[l], b_router[l],
                 w_e_in[l], b_e_in[l], w_e_out[l], b_e_out[l])
        xp, sp = trunk_layer(xp, c_prompt, lambda h: mixer_prompt(h, *mix_w), *ffn_w)
        xs, ss = trunk_layer(
            xs, c_sample,
            lambda h: mixer_sample(h, cache_a_k[l], cache_a_v[l], cache_b_k[l], cache_b_v[l],
                                   state_conv[l], *mix_w),
            *ffn_w)
        states_p.append(sp)
        states_s.append(ss)
    a_k_p, a_v_p, b_k_p, b_v_p, conv_p = (jnp.stack(z) for z in zip(*states_p))
    a_k_s, a_v_s, b_k_s, b_v_s, conv_s = (jnp.stack(z) for z in zip(*states_s))
    return (xp, xs, a_k_p, a_v_p, b_k_p, b_v_p, conv_p, a_k_s, a_v_s, b_k_s, b_v_s, conv_s)


_drawn_inputs = setup_inputs


def setup_inputs(seed=0):
    import zlib

    import numpy as np

    out = dict(_drawn_inputs(seed))
    spreads = {}
    factors = {'rel_bias_a': 47.662,
     't5_bias': 38.113,
     'sinks': 64.0,
     'conv_b': 8.0,
     'conv_ln_g': 8.0,
     'conv_ln_b': 48.296,
     'b_router': 32.351,
     'b_e_in': 29.338,
     'b_e_out': 21.685}
    for name, (base, spread) in spreads.items():
        noise = np.random.default_rng([zlib.crc32(name.encode()), seed]).standard_normal(out[name].shape)
        drawn = base * np.exp(spread * noise) if base else spread * noise
        out[name] = jnp.asarray(drawn.astype(out[name].dtype))
    for name, factor in factors.items():
        out[name] = (out[name] * factor).astype(out[name].dtype)
    return out
```

```python
import math
from contextlib import ExitStack

import numpy as np
import concourse.bass as bass
from concourse import mybir

F32 = mybir.dt.float32
BF16 = mybir.dt.bfloat16
I32 = mybir.dt.int32
ALU = mybir.AluOpType
ACT = mybir.ActivationFunctionType
AX_X = mybir.AxisListType.X

P = 128
D = 1024
DK = D // P
SEQ, DEC, PAST = 256, 32, 256
NTOK = SEQ + DEC
TS = [128, 128, 32]
T0 = [0, 128, 256]
GROUP = [0, 0, 1]
CHUNK = 64
HD = 64
SCALE = HD ** -0.5
AH, BH = 4, 8
A_CLIP = 128
BCACHE = 128
SA_K, SB_K = PAST + DEC, BCACHE + DEC
T5_BUCKETS, T5_MAX = 32, 128
C_CH = 256
CONV_W = 31
PADW = CONV_W - 1
U_S = PADW + SEQ
U_LEN = U_S + PADW + DEC
Y_LEN = U_LEN - PADW
NE, TOPK = 32, 4
SLOTS = 64
LIMIT = 7.0
SW_ALPHA = 1.702
ALPHA = 2 ** 0.25
EPS = 1e-5
NEG = -1e30
EXT = 512
EXT_0 = 384


def t5_runs():
    rel = np.arange(EXT) - EXT_0
    nb = T5_BUCKETS // 2
    exact = nb // 2
    n = np.abs(rel)
    nf = np.maximum(n, 1).astype(np.float32)
    large = exact + (np.log(nf / exact) / math.log(T5_MAX / exact) * (nb - exact)).astype(np.int32)
    large = np.minimum(large, nb - 1)
    bucket = np.where(rel > 0, nb, 0) + np.where(n < exact, n, large)
    cuts = [0] + [j for j in range(1, EXT) if bucket[j] != bucket[j - 1]] + [EXT]
    return [(a, b, int(bucket[a])) for a, b in zip(cuts, cuts[1:])]


def hybrid_streaming_encoder_step(nc, x_prompt, x_sample, cache_a_k, cache_a_v, cache_b_k, cache_b_v, state_conv,
                                  c_prompt, c_sample, w_in, w_out, rel_bias_a, t5_bias, sinks, conv_w, conv_b,
                                  conv_ln_g, conv_ln_b, w_ada, b_ada, ln_g, ln_b, w_router, b_router,
                                  w_e_in, b_e_in, w_e_out, b_e_out,
                                  y_prompt, y_sample, o_ak_p, o_av_p, o_bk_p, o_bv_p, o_conv_p,
                                  o_ak_s, o_av_s, o_bk_s, o_bv_s, o_conv_s,
                                  mod_dram, ext_dram, x1_dram):
    with ExitStack() as ctx:
        def sb(name, shape, dt=F32):
            return ctx.enter_context(nc.sbuf_tensor(name, shape, dt))

        def sem(name):
            return ctx.enter_context(nc.semaphore(name))

        W1 = [sb("w1_even", [P, DK * 2 * D]), sb("w1_odd", [P, DK * 2 * D])]
        W2 = sb("w2", [P, DK * D])
        w1v = [w[:, :].rearrange("p (k n) -> p k n", k=DK) for w in W1]
        w2v = W2[:, :].rearrange("p (k n) -> p k n", k=DK)
        XY = sb("xy", [P, 3, D])
        HB = sb("hb", [P, 3584])
        B3 = sb("b3", [96, 3 * D], BF16)
        MT = sb("mt", [P, 4096])

        hT = MT[:, 0:2304].rearrange("p (k t) -> p k t", k=DK)
        h2row = MT[:, 2304:3328]
        modr = MT[0:34, 2304:3328].rearrange("p (s n) -> p s n", s=2)
        bada = XY[64:98, 2, :].rearrange("p (s n) -> p s n", s=2)
        va_c = MT[:, 3328:3840].rearrange("p (t c) -> p t c", t=2)
        vb_c = MT[:, 3840:3968]
        xT, glu, gsig, sg, act, aT, outb, lin = (MT[:, 512 * j:512 * (j + 1)] for j in range(8))

        hb = HB[:, 0:3072].bitcast(BF16).rearrange("p (t j d) -> p t j d", t=2, j=3)
        hb_s = HB[:, 3072:3584].bitcast(BF16)
        prob = HB[:, 0:1024].rearrange("p (s h k) -> p s h k", s=2, h=2)
        pT = HB[:, 1024:1536]
        bias_sa = HB[:, 1536:1824]
        bias_sb = HB[:, 1824:2144].rearrange("p (n k) -> p n k", n=2)
        kT_s = HB[:, 2144:2720].rearrange("p (j k) -> p j k", j=2)
        kbT_s = HB[:, 2720:2880]
        zrow = HB[:, 0:768].rearrange("p (t c) -> p t c", t=3)
        zsig = HB[:, 768:1536].rearrange("p (t c) -> p t c", t=3)

        ring = W1[1][:, 0:8192].rearrange("p (s k n) -> p s k n", s=2, k=4)
        qkT = W1[1][:, 8192:10784].rearrange("p (j t) -> p j t", j=9)
        vtok = W1[1][:, 10784:11936].rearrange("p (t c) -> p t c", t=3)
        ktok = W1[1][:, 11936:13088].rearrange("p (t c) -> p t c", t=3)
        bias_b = W1[1][:, 13088:15136].rearrange("p (h k) -> p h k", h=BH)
        bias_a = W1[1][:, 15136:16160].rearrange("p (h k) -> p h k", h=AH)
        g1b = W1[1][:, 0:2048].rearrange("p (g d) -> p g d", g=2)
        sh2b = W1[1][:, 2048:4096].rearrange("p (g d) -> p g d", g=2)
        sc2b = W1[1][:, 4096:6144].rearrange("p (g d) -> p g d", g=2)
        lng = W1[1][:, 6144:7168]
        lnb = W1[1][:, 7168:8192]
        hb_mid = W1[1][0:32, 15136:15648].bitcast(BF16)
        h2rows = [h2row, W1[1][:, 13088:14112], W1[1][:, 14112:15136]]

        cs = W2[0:64, 0:256]
        ka_c = W2[:, 256:768].rearrange("p (t c) -> p t c", t=2)
        kb_c = W2[:, 768:896]
        uext = W2[:, 896:1592].rearrange("p (c t) -> p c t", c=2)
        yconv = W2[:, 1592:2228].rearrange("p (c t) -> p c t", c=2)
        clg = W2[:, 2228:2484]
        clb = W2[:, 2484:2740]
        ust = W2[0:PADW, 2740:3252].rearrange("p (g c) -> p g c", g=2)
        be_src = W2[0:32, 3252:6324]
        be_res = W2[0:32, 6324:7348]
        be_mid = W2[0:32, 7348:7860].bitcast(BF16)

        x1_fin = W1[0][:, 0:3072].rearrange("p (t d) -> p t d", t=3)
        g2b = W1[0][:, 3072:5120].rearrange("p (g d) -> p g d", g=2)
        lng2 = W1[0][:, 5120:6144]
        lnb2 = W1[0][:, 6144:7168]

        ident = sb("ident", [P, P])
        anti = sb("anti", [P, P])
        anti32 = sb("anti32", [P, P])
        upper = sb("upper", [P, P], BF16)
        ones = sb("ones", [P, P], BF16)
        eye3 = sb("eye3", [96, NE], BF16)
        iota = sb("iota", [P, 5 * 2 * SLOTS])
        cT = sb("cT", [P, 2, DK])
        scT = sb("scT", [P, DK, 2])
        csig = sb("csig", [P, 2, DK])
        modc = sb("modc", [P, 2, 2, DK])
        tabA = sb("tabA", [AH, 2 * A_CLIP + 1])
        tabB = sb("tabB", [BH, T5_BUCKETS])
        cwT = sb("cwT", [P, 2, 32])
        cbc = sb("cbc", [P, 2])
        nsink = sb("nsink", [P, BH])
        nsink_s = sb("nsink_s", [P, 2])
        stat = sb("stat", [P, 2, 2])
        dsink = sb("dsink", [P, 2, 2])
        esum = sb("esum", [P, 2, 2])
        esink = sb("esink", [P, 2, 2])
        rinv = sb("rinv", [P, 2])
        mx = sb("mx", [P, 2])
        bnst = sb("bnst", [P, 2, 6])
        bnmv = sb("bnmv", [P, 2])
        rstd = sb("rstd", [P, 1])
        wr = sb("wr", [P, DK, NE])
        brb = sb("brb", [P, NE])
        lg = sb("lg", [P, 3, NE])
        top8 = sb("top8", [P, 8])
        rt = sb("rt", [P, 4, NE])
        rs = sb("rs", [P, 4])
        maskb = sb("maskb", [P, 3, NE], BF16)
        maskf = sb("maskf", [P, 3, NE])
        gate = sb("gate", [P, 3, NE])
        rank = sb("rank", [P, 3, NE])
        cnt = sb("cnt", [1, 4, NE])
        cumf = sb("cumf", [1, NE + 3])
        cum = sb("cum", [1, NE + 3], I32)
        rkc = sb("rkc", [P, 3, 1])
        gtc = sb("gtc", [P, 3, 1])
        cstat = sb("cstat", [P, 3, 2])
        cstd = sb("cstd", [P, 3])
        sel = sb("sel", [96, 2, SLOTS], BF16)
        pick = sb("pick", [P, 3, SLOTS], BF16)
        gpick = sb("gpick", [P, 3, 2 * SLOTS])
        gpickT = sb("gpickT", [P, NTOK])

        bank = [ctx.enter_context(nc.psum_tensor(f"bank{j}", [P, 512], F32)) for j in range(8)]

        ld = {n: sem(f"ld_{n}") for n in (
            "c", "x", "cs", "ka", "kb", "v", "tabs", "cb", "cln", "sinks", "be", "wr", "ext", "toep", "wout",
            "brow", "final", "x1s")}
        ld_win = [sem(f"ld_win{j}") for j in range(4)]
        ld_ada = [sem("ld_ada0"), sem("ld_ada1")]
        ld_bada = [sem("ld_bada0"), sem("ld_bada1")]
        ld_glu = [sem("ld_glu_even"), sem("ld_glu_odd")]
        ld_lin = [sem("ld_lin_even"), sem("ld_lin_odd")]
        ld_w2 = sem("ld_w2")
        st_mod = [sem("st_mod0"), sem("st_mod1")]
        st_out = sem("st_out")
        pool_chain, dve_chain, act_chain = sem("pool_chain"), sem("dve_chain"), sem("act_chain")
        consts_done, b3_done, ext_done, masks_done, cs_zero = (
            sem(n) for n in ("consts_done", "b3_done", "ext_done", "masks_done", "cs_zero"))
        csig_done, scT_done = sem("csig_done"), sem("scT_done")
        ada_done, mod_ready = sem("ada_done"), sem("mod_ready")
        tr_done, tr_used = sem("tr_done"), sem("tr_used")
        h1_ready = sem("h1_ready")
        proj_done, proj_used, gate_sig, u_ready = (sem(n) for n in ("proj_done", "proj_used", "gate_sig", "u_ready"))
        qk_copied = sem("qk_copied")
        conv_done, conv_var, conv_std, conv_z, conv_sig, conv_out = (
            sem(n) for n in ("conv_done", "conv_var", "conv_std", "conv_z", "conv_sig", "conv_out"))
        u_gated = sem("u_gated")
        kt_ready, ust_ready, ust_sent = sem("kt_ready"), sem("ust_ready"), sem("ust_sent")
        keys_ready = sem("keys_ready")
        log_done, negm_done, exp_done, prob_done = (sem(n) for n in ("log_done", "negm_done", "exp_done", "prob_done"))
        pT_done, pT_copied, o_done, o_copied = (sem(n) for n in ("pT_done", "pT_copied", "o_done", "o_copied"))
        op_done, op_used, ln_var, ln_std, x1_ready, h2_ready = (
            sem(n) for n in ("op_done", "op_used", "ln_var", "ln_std", "x1_ready", "h2_ready"))
        part1, part2, part3, res1, res2 = (sem(n) for n in ("part1", "part2", "part3", "res1", "res2"))
        h2T_done, h2T_copied, lg_done, mask_done, rank_done, cum_ready = (
            sem(n) for n in ("h2T_done", "h2T_copied", "lg_done", "mask_done", "rank_done", "cum_ready"))
        y_zero, moe_zero = sem("y_zero"), sem("moe_zero")
        m = {n: sem(f"m_{n}") for n in (
            "cur", "pick", "gath_a", "gath_b", "xT_a", "xT_b", "G", "glu", "sig", "gs", "c01", "y01", "L", "lin_a", "lin",
            "act_a", "act", "c2", "y2", "gT", "gT_copied", "T_a", "T_b", "aT_a", "aT_b", "S2", "out")}
        sel_ready, cur_ready, top_done, gexp_done = (sem(n) for n in ("sel_ready", "cur_ready", "top_done", "gexp_done"))
        fin_c, fin_y, fin_var, fin_std, fin_ready = (
            sem(n) for n in ("fin_c", "fin_y", "fin_var", "fin_std", "fin_ready"))

        block = ctx.enter_context(nc.Block())

        ATT = [("A", t, j) for t in range(2) for j in range(2)] + [("B", t, i) for t in range(2) for i in range(4)] \
            + [("SA", 2, 0), ("SB", 2, 0), ("SB", 2, 1)]
        NATT = len(ATT)
        PROJ = ["gg0", "ga0", "gg1", "ga1", "k0", "k1", "q0", "q1", "qb0", "qb1", "qb2", "qb3", "kb"]
        PIECE = {"g": 0, "k": 1, "q": 1, "qb": 2, "kb": 3}
        QK_AT = {"q0": 0, "q1": 1, "k0": 2, "k1": 3, "qb0": 4, "qb1": 5, "qb2": 6, "qb3": 7, "kb": 8}
        NPROJ = len(PROJ) + 3
        W_K, W_VA, W_QB, W_KB, W_VB, W_G = 256, 512, 768, 1280, 1408, 1536
        J_CS, J_KA, J_KB = 0, 1, 2
        J_M = 3
        J_H = 4
        J_Y = J_H + 6
        J_KT = J_Y + 2
        J_U = J_KT + 3
        J_Z = J_U + 1
        J_H2 = J_Z + 2
        N_OUT = 4 + 4 + 4 + 3

        def block_range(eng, i, p):
            lo = eng.value_load(cum[0:1, bass.ds(2 * i + p + 2, 1)], min_val=0, max_val=160)
            hi = eng.value_load(cum[0:1, bass.ds(2 * i + p + 3, 1)], min_val=1, max_val=160)
            return lo, hi

        def exps_through(s):
            return sum((1 if t == 2 else 2) + (kind in ("B", "SB")) for kind, t, _ in ATT[:s + 1])

        def probs_through(s):
            return sum(1 if t == 2 else 2 for _, t, _ in ATT[:s + 1])

        def logit_bank(s, h):
            return bank[(4, 2)[h] + s % 2]

        def keys_of(kind, t):
            return {"SA": SA_K, "SB": SB_K}.get(kind, P * (t + 1))

        @block.sync
        def _(sp):
            def ada_unit(u):
                pair, half = divmod(u, 2)
                if u >= 2:
                    sp.wait_ge(ada_done, u - 1)
                sp.dma_start(ring[:, u % 2], w_ada[0, 512 * half:512 * (half + 1), D * pair:D * (pair + 1)]
                             .rearrange("(k p) n -> p k n", p=P)).then_inc(ld_ada[u % 2], 16)
                if half == 0:
                    if pair >= 2:
                        sp.wait_ge(mod_ready, pair - 1)
                    for j in range(2):
                        src = b_ada[0:1, D * pair + 512 * j:D * pair + 512 * (j + 1)].to_broadcast([2, 512])
                        sp.dma_start(bada[32 * j:32 * j + 2, pair % 2, :], src).then_inc(ld_bada[pair % 2], 16)

            for u in range(4):
                ada_unit(u)
            wi = w_in[0].rearrange("(k p) n -> p k n", p=P)
            win = w1v[0]
            for piece, cols in ((0, [(W_G, 2048)]), (1, [(0, 512)]), (2, [(W_QB, W_KB)]), (3, [(W_VA, W_QB), (W_KB, W_G)])):
                for a, b in cols:
                    if piece == 2:
                        for h in range(BH):
                            to = a + HD * (2 * (h % 4) + h // 4)
                            sp.dma_start(win[:, :, to:to + HD], wi[:, :, a + HD * h:a + HD * (h + 1)]).then_inc(ld_win[piece], 16)
                    else:
                        sp.dma_start(win[:, :, a:b], wi[:, :, a:b]).then_inc(ld_win[piece], 16)
            for u in range(4, 12):
                ada_unit(u)
            sp.wait_ge(ust_sent, 32)
            sp.wait_ge(conv_z, 1)
            sp.wait_ge(b3_done, 1)
            wo = w_out[0]
            for j in (0, 1):
                sp.dma_start(w2v[:, j, :], wo[P * j:P * (j + 1), :]).then_inc(ld["wout"], 16)
            for hf in range(2):
                sp.dma_start(w2v[64 * hf:64 * hf + 64, 2:6, :], wo[256 + 256 * hf:512 + 256 * hf, :]
                             .rearrange("(i p) n -> p i n", p=64)).then_inc(ld["wout"], 16)
            for j in (6, 7):
                sp.dma_start(w2v[:, j, :], wo[P * j:P * (j + 1), :]).then_inc(ld["wout"], 16)
            sp.wait_ge(ada_done, 12)
            sp.wait_ge(st_mod[0], 2 * 32)
            sp.wait_ge(st_mod[1], 2 * 32)
            for dst, at in ((g1b, 2), (sh2b, 3), (sc2b, 4)):
                sp.dma_start(dst[:, 0, :], mod_dram[0:1, D * at:D * (at + 1)].to_broadcast([P, D])).then_inc(ld["brow"], 16)
                sp.dma_start(dst[0:32, 1, :], mod_dram[1:2, D * at:D * (at + 1)].to_broadcast([32, D])).then_inc(ld["brow"], 16)
            sp.dma_start(lng, ln_g[0, 0:1, :].to_broadcast([P, D])).then_inc(ld["brow"], 16)
            sp.dma_start(lnb, ln_b[0, 0:1, :].to_broadcast([P, D])).then_inc(ld["brow"], 16)

            def load_w1(par, e, half):
                src = w_e_in[0, e] if isinstance(e, int) else w_e_in[0, bass.ds(e, 1)].rearrange("a d n -> (a d) n")
                src = src.rearrange("(k p) n -> p k n", p=P)
                c = slice(D * half, D * (half + 1))
                for j in range(2):
                    sp.dma_start(w1v[par][:, 4 * j:4 * j + 4, c], src[:, 4 * j:4 * j + 4, c]).then_inc((ld_glu, ld_lin)[half][par], 16)

            def load_w2(e):
                src = w_e_out[0, e] if isinstance(e, int) else w_e_out[0, bass.ds(e, 1)].rearrange("a d n -> (a d) n")
                src = src.rearrange("(k p) n -> p k n", p=P)
                for j in range(2):
                    sp.dma_start(w2v[:, 4 * j:4 * j + 4, :], src[:, 4 * j:4 * j + 4, :]).then_inc(ld_w2, 16)

            sp.wait_ge(proj_done, NPROJ)
            load_w1(0, 0, 0)
            load_w1(0, 0, 1)
            sp.wait_ge(op_done, 3)
            load_w2(0)
            sp.wait_ge(h2_ready, 3)
            sp.wait_ge(part3, 3)
            sp.wait_ge(st_out, 16 * (N_OUT - 3))
            load_w1(1, 1, 0)
            load_w1(1, 1, 1)
            sp.wait_ge(cum_ready, 1)

            def freed(e):
                return sp.snap(sp.value_load(cum[0:1, bass.ds(e + 3, 1)], min_val=1, max_val=160) + 1,
                               min_val=2, max_val=161)

            with sp.Fori(0, NE // 2 - 1) as i:
                v = freed(2 * i)
                w = freed(2 * i + 1)
                sp.wait_ge(m["G"], v)
                load_w1(0, 2 * i + 2, 0)
                sp.wait_ge(m["L"], v)
                load_w1(0, 2 * i + 2, 1)
                sp.wait_ge(m["S2"], v)
                load_w2(2 * i + 1)
                sp.wait_ge(m["G"], w)
                load_w1(1, 2 * i + 3, 0)
                sp.wait_ge(m["L"], w)
                load_w1(1, 2 * i + 3, 1)
                sp.wait_ge(m["S2"], w)
                load_w2(2 * i + 2)
            v = sp.snap(sp.value_load(cum[0:1, NE + 1:NE + 2], min_val=1, max_val=160) + 1, min_val=2, max_val=161)
            sp.wait_ge(m["S2"], v)
            load_w2(NE - 1)
            for t in range(3):
                sp.dma_start(x1_fin[0:TS[t], t, :], x1_dram[T0[t]:T0[t] + TS[t], :]).then_inc(ld["final"], 16)
            sp.dma_start(g2b[:, 0, :], mod_dram[0:1, 5 * D:6 * D].to_broadcast([P, D])).then_inc(ld["final"], 16)
            sp.dma_start(g2b[0:32, 1, :], mod_dram[1:2, 5 * D:6 * D].to_broadcast([32, D])).then_inc(ld["final"], 16)
            sp.dma_start(lng2, ln_g[0, 1:2, :].to_broadcast([P, D])).then_inc(ld["final"], 16)
            sp.dma_start(lnb2, ln_b[0, 1:2, :].to_broadcast([P, D])).then_inc(ld["final"], 16)
            for t in range(3):
                sp.wait_ge(fin_ready, t + 1)
                dst = y_prompt[0, T0[t]:T0[t] + P, :] if t < 2 else y_sample[0]
                sp.dma_start(dst, x1_fin[0:TS[t], t, :]).then_inc(st_out, 16)
            sp.wait_ge(st_out, 16 * N_OUT)

        @block.gpsimd
        def _(pool):
            count = [0]

            def link(ins):
                count[0] += 1
                ins.then_inc(pool_chain, 1)
                pool.wait_ge(pool_chain, count[0])

            g = nc.gpsimd
            g.memset(cs, 0.0).then_inc(cs_zero, 1)
            for tile in (ident, anti, anti32):
                link(g.memset(tile[:, :], 0.0))
            link(g.memset(upper[:, :], 1.0))
            link(g.memset(eye3[:, :], 0.0))
            g.memset(ones[:, :], 1.0).then_inc(consts_done, 1)
            link(g.affine_select(out=ident[:, :], in_=ident[:, :], compare_op=ALU.not_equal, fill=1.0, base=0,
                                 pattern=[[-1, P]], channel_multiplier=1))
            link(g.affine_select(out=anti[:, :], in_=anti[:, :], compare_op=ALU.not_equal, fill=1.0, base=-(P - 1),
                                 pattern=[[1, P]], channel_multiplier=1))
            a32 = anti32[:, :].rearrange("p (b j) -> p b j", b=4)
            link(g.affine_select(out=a32, in_=a32, compare_op=ALU.not_equal, fill=1.0, base=-31,
                                 pattern=[[-32, 4], [1, 32]], channel_multiplier=1))
            link(g.affine_select(out=upper[:, :], in_=upper[:, :], compare_op=ALU.is_ge, fill=0.0, base=-1,
                                 pattern=[[1, P]], channel_multiplier=-1))
            for j in range(3):
                link(g.affine_select(out=eye3[:, :], in_=eye3[:, :], compare_op=ALU.not_equal, fill=1.0, base=-32 * j,
                                     pattern=[[-1, NE]], channel_multiplier=1))
            g.iota(iota[:, :], pattern=[[SLOTS, 5], [0, 2], [1, SLOTS]], base=0, channel_multiplier=0,
                   allow_small_or_imprecise_dtypes=True).then_inc(consts_done, 1)
            extA = MT[0:AH, 0:EXT]
            extB = MT[0:BH, EXT:2 * EXT]
            pool.wait_ge(ld["tabs"], 32)
            g.tensor_copy(extA[:, 0:256], tabA[:, 0:1].to_broadcast([AH, 256])).then_inc(ext_done, 1)
            g.tensor_copy(extA[:, 256:512], tabA[:, 0:256]).then_inc(ext_done, 1)
            for a, b, bk in t5_runs():
                g.tensor_copy(extB[:, a:b], tabB[:, bk:bk + 1].to_broadcast([BH, b - a])).then_inc(ext_done, 1)
            g.memset(uext[:, :, 0:PADW], 0.0).then_inc(masks_done, 1)
            pool.wait_ge(ld["be"], 32)
            for j in range(3):
                c = slice(D * j, D * (j + 1))
                link(g.tensor_copy(B3[0:32, c], be_src[:, c]))
                link(g.tensor_tensor(be_res, be_src[:, c], B3[0:32, c], ALU.subtract))
                link(g.tensor_copy(be_mid, be_res))
                link(g.tensor_copy(B3[32:64, c], be_mid))
                link(g.tensor_tensor(be_res, be_res, be_mid, ALU.subtract))
                ins = g.tensor_copy(B3[64:96, c], be_res)
                link(ins)
            pool.wait_ge(ld["toep"], 10 * 16)
            g.memset(bias_a[64:128, :, 192:256], NEG).then_inc(masks_done, 1)
            g.memset(bias_b[64:128, :, 192:256], NEG).then_inc(masks_done, 1)
            g.memset(bias_b[0:64, :, 0:64], NEG).then_inc(masks_done, 1)
            g.sem_inc(b3_done, 1)
            for t in range(3):
                n = TS[t]
                pool.wait_ge(part1, t + 1)
                first = hb[0:n, t, 0, :] if t < 2 else hb_s[0:32, :]
                g.tensor_tensor(h2rows[t][0:n, :], h2rows[t][0:n, :], first, ALU.subtract).then_inc(res1, 1)
            for t in range(3):
                n = TS[t]
                pool.wait_ge(part2, t + 1)
                pool.wait_ge(res1, t + 1)
                second = hb[0:n, t, 1, :] if t < 2 else hb_mid
                g.tensor_tensor(h2rows[t][0:n, :], h2rows[t][0:n, :], second, ALU.subtract).then_inc(res2, 1)

        @block.scalar
        def _(eng):
            count = [0]
            a = nc.scalar

            def link(ins):
                count[0] += 1
                ins.then_inc(act_chain, 1)
                eng.wait_ge(act_chain, count[0])

            eng.dma_start(cT[:, 0, :], c_prompt[0].rearrange("(k p) -> p k", p=P), allow_slow_non_contiguous=True).then_inc(ld["c"], 16)
            eng.dma_start(cT[:, 1, :], c_sample[0].rearrange("(k p) -> p k", p=P), allow_slow_non_contiguous=True).then_inc(ld["c"], 16)
            eng.wait_ge(cs_zero, 1)
            eng.dma_start(cs[0:CONV_W, :], conv_w[0]).then_inc(ld["cs"], 16)
            eng.dma_start(cs[32:32 + PADW, :], state_conv[0, 0]).then_inc(ld["cs"], 16)
            eng.dma_start(tabA[:, :], rel_bias_a[0].rearrange("r h -> h r"), allow_slow_non_contiguous=True).then_inc(ld["tabs"], 16)
            eng.dma_start(tabB[:, :], t5_bias.rearrange("r h -> h r"), allow_slow_non_contiguous=True).then_inc(ld["tabs"], 16)
            eng.dma_start(ka_c, cache_a_k[0, 0].rearrange("(t p) h d -> p t (h d)", p=P)).then_inc(ld["ka"], 16)
            eng.dma_start(kb_c, cache_b_k[0, 0].rearrange("p h d -> p (h d)")).then_inc(ld["kb"], 16)
            eng.dma_start(XY[:, 0:2, :], x_prompt[0].rearrange("(t p) d -> p t d", p=P)).then_inc(ld["x"], 16)
            eng.dma_start(XY[0:32, 2, :], x_sample[0]).then_inc(ld["x"], 16)
            eng.dma_start(cbc[:, :], conv_b[0].rearrange("(k p) -> p k", p=P), allow_slow_non_contiguous=True).then_inc(ld["cb"], 16)
            eng.dma_start(clg, conv_ln_g[0:1, :].to_broadcast([P, C_CH])).then_inc(ld["cln"], 16)
            eng.dma_start(clb, conv_ln_b[0:1, :].to_broadcast([P, C_CH])).then_inc(ld["cln"], 16)
            eng.dma_start(nsink[:, :], sinks[0:1, :].to_broadcast([P, BH])).then_inc(ld["sinks"], 16)
            for i in range(4):
                for n in range(2):
                    eng.dma_start(nsink_s[32 * i:32 * i + 32, n:n + 1], sinks[0:1, 4 * n + i:4 * n + i + 1].to_broadcast([32, 1]))\
                       .then_inc(ld["sinks"], 16)
            eng.dma_start(be_src[:, 0:2 * D], b_e_in[0]).then_inc(ld["be"], 16)
            eng.dma_start(be_src[:, 2 * D:3 * D], b_e_out[0]).then_inc(ld["be"], 16)
            eng.dma_start(va_c, cache_a_v[0, 0].rearrange("(t p) h d -> p t (h d)", p=P)).then_inc(ld["v"], 16)
            eng.dma_start(vb_c, cache_b_v[0, 0].rearrange("p h d -> p (h d)")).then_inc(ld["v"], 16)
            eng.dma_start(wr[:, :, :], w_router[0].rearrange("(k p) e -> p k e", p=P)).then_inc(ld["wr"], 16)
            eng.dma_start(brb[:, :], b_router[0:1, :].to_broadcast([P, NE])).then_inc(ld["wr"], 16)
            for src, dst, n in ((cache_a_k, o_ak_s, PAST), (cache_a_v, o_av_s, PAST), (cache_b_k, o_bk_s, BCACHE), (cache_b_v, o_bv_s, BCACHE)):
                eng.dma_start(dst[0, 0, 0:n - DEC].rearrange("p h d -> p (h d)"), src[0, 0, DEC:n].rearrange("p h d -> p (h d)"))\
                   .then_inc(st_out, 16)

            eng.wait_ge(ld["c"], 32)
            a.activation(csig[:, :, :], cT[:, :, :], ACT.Sigmoid).then_inc(csig_done, 1)
            eng.wait_ge(ext_done, 2 + len(t5_runs()))
            eng.dma_start(ext_dram[0:AH, :], MT[0:AH, 0:EXT]).then_inc(ld["ext"], 16)
            eng.dma_start(ext_dram[AH:AH + BH, :], MT[0:BH, EXT:2 * EXT]).then_inc(ld["ext"], 16)
            eng.wait_ge(ld["ext"], 32)

            def toeplitz(first_row, start, rows, heads, step, keys):
                return bass.AP(tensor=ext_dram.tensor, offset=ext_dram.offset + first_row * EXT + start,
                               ap=[[1, rows], [step * EXT, heads], [1, keys]])

            eng.dma_start(bias_a, toeplitz(0, EXT_0 - 255, P, AH, 1, 256)).then_inc(ld["toep"], 16)
            eng.dma_start(bias_b, toeplitz(AH, EXT_0 - 255, P, BH, 1, 256)).then_inc(ld["toep"], 16)
            for i in range(4):
                eng.dma_start(bias_sa[32 * i:32 * i + 32, :], bass.AP(tensor=ext_dram.tensor, offset=ext_dram.offset + i * EXT + EXT_0 - PAST - 31,
                              ap=[[1, 32], [1, SA_K]])).then_inc(ld["toep"], 16)
                eng.dma_start(bias_sb[32 * i:32 * i + 32, :, :], toeplitz(AH + i, EXT_0 - BCACHE - 31, 32, 2, 4, SB_K)).then_inc(ld["toep"], 16)
            def store_mod(pair):
                eng.wait_ge(mod_ready, pair + 1)
                for j in range(2):
                    eng.dma_start(mod_dram[:, D * pair + 512 * j:D * pair + 512 * (j + 1)], modr[32 * j:32 * j + 2, pair % 2, :])\
                       .then_inc(st_mod[pair % 2], 16)


            for n, name in enumerate(PROJ + ["v0", "v1", "v2"]):
                eng.wait_ge(proj_done, n + 1)
                ps = bank[4 + n % 2]
                if name[:2] == "gg":
                    ins = a.activation(yconv[:, int(name[2]), 0:NTOK], ps[:, 0:NTOK], ACT.Sigmoid)
                elif name[:2] == "ga":
                    c = int(name[2])
                    link(a.activation(uext[:, c, PADW:U_S], ps[:, 0:SEQ], ACT.Copy))
                    ins = a.activation(uext[:, c, U_S + PADW:U_LEN], ps[:, SEQ:NTOK], ACT.Copy)
                elif name[0] == "v":
                    t = int(name[1])
                    ins = a.activation(vtok[0:TS[t], t, :], ps[0:TS[t], 0:384], ACT.Copy)
                else:
                    scale = SCALE if name[0] == "q" else 1.0
                    ins = a.activation(qkT[:, QK_AT[name], :], ps[:, 0:NTOK], ACT.Copy, scale=scale)
                ins.then_inc(proj_used, 1)

            eng.wait_ge(conv_var, 1)
            a.activation(cstd[:, :], cstat[:, :, 1], ACT.Sqrt).then_inc(conv_std, 1)
            eng.wait_ge(conv_z, 1)
            for t in range(3):
                a.activation(zsig[0:TS[t], t, :], zrow[0:TS[t], t, :], ACT.Sigmoid).then_inc(conv_sig, 1)

            def dma_out(dst, src):
                eng.dma_start(dst, src).then_inc(st_out, 16)

            dma_out(o_av_p[0, 0].rearrange("(t p) h d -> p t (h d)", p=P), vtok[:, 0:2, 0:256])
            dma_out(o_bv_p[0, 0].rearrange("p h d -> p (h d)"), vtok[:, 1, 256:384])
            dma_out(o_av_s[0, 0, PAST - DEC:PAST].rearrange("p h d -> p (h d)"), vtok[0:32, 2, 0:256])
            dma_out(o_bv_s[0, 0, BCACHE - DEC:BCACHE].rearrange("p h d -> p (h d)"), vtok[0:32, 2, 256:384])
            eng.wait_ge(kt_ready, 3)
            dma_out(o_ak_p[0, 0].rearrange("(t p) h d -> p t (h d)", p=P), ktok[:, 0:2, 0:256])
            dma_out(o_bk_p[0, 0].rearrange("p h d -> p (h d)"), ktok[:, 1, 256:384])
            dma_out(o_ak_s[0, 0, PAST - DEC:PAST].rearrange("p h d -> p (h d)"), ktok[0:32, 2, 0:256])
            dma_out(o_bk_s[0, 0, BCACHE - DEC:BCACHE].rearrange("p h d -> p (h d)"), ktok[0:32, 2, 256:384])
            eng.wait_ge(ust_ready, 1)
            for dst, g in ((o_conv_p, 0), (o_conv_s, 1)):
                eng.dma_start(dst[0, 0], ust[:, g, :]).then_inc(ust_sent, 16)

            def exps(s):
                kind, t, j = ATT[s]
                nk = keys_of(kind, t)
                nh = 1 if t == 2 else 2
                eng.wait_ge(negm_done, s + 1)
                if s == 0:
                    eng.wait_ge(tr_used, J_Z + 2)
                if s >= 2:
                    eng.wait_ge(pT_done, s - 1)
                pr = prob[:, s % 2, :, :] if nh == 2 else prob[:, s % 2, :, :].rearrange("p h k -> p (h k)").unsqueeze(1)
                for h in range(nh):
                    a.activation(pr[:, h, 0:nk], logit_bank(s, h)[:, 0:nk], ACT.Exp, bias=stat[:, s % 2, h:h + 1],
                                 accum_out=esum[:, s % 2, h:h + 1]).then_inc(exp_done, 1)
                if kind in ("B", "SB"):
                    a.activation(esink[:, s % 2, 0:nh], dsink[:, s % 2, 0:nh], ACT.Exp).then_inc(exp_done, 1)

            def copy_pT(s):
                kind, t, j = ATT[s]
                nk = keys_of(kind, t)
                eng.wait_ge(pT_done, s + 1)
                if s >= 1:
                    eng.wait_ge(o_done, s)
                if t < 2:
                    w = 2 * P * (t + 1)
                    a.activation(pT[:, 0:w], bank[6][:, 0:w], ACT.Copy).then_inc(pT_copied, 1)
                else:
                    w = nk // P * P
                    link(a.activation(pT[:, 0:w], bank[6][:, 0:w], ACT.Copy))
                    a.activation(pT[0:32, w:w + P], bank[6][0:32, w:w + P], ACT.Copy).then_inc(pT_copied, 1)

            exps(0)
            for s in range(NATT):
                if s + 1 < NATT:
                    exps(s + 1)
                copy_pT(s)
                if s in (1, 3, 5, 7):
                    store_mod(2 + s // 2)

            for t in range(3):
                n = TS[t]
                eng.wait_ge(ln_var, t + 1)
                a.activation(rstd[0:n, :], bnmv[0:n, 1:2], ACT.Sqrt).then_inc(ln_std, 1)
                eng.wait_ge(x1_ready, t + 1)
                eng.dma_start(x1_dram[T0[t]:T0[t] + n, :], XY[0:n, t, :]).then_inc(ld["x1s"], 16)
                for j in range(2):
                    eng.wait_ge(h2T_done, 2 * t + j + 1)
                    a.activation(hT[:, 4 * j:4 * j + 4, T0[t]:T0[t] + n],
                                 bank[2 + j][:, :].rearrange("p (k t) -> p k t", k=4)[:, :, 0:n], ACT.Copy).then_inc(h2T_copied, 1)
                first = hb[0:n, t, 0, :] if t < 2 else hb_s[0:32, :]
                a.activation(first, h2rows[t][0:n, :], ACT.Copy).then_inc(part1, 1)
            for t in range(3):
                eng.wait_ge(res1, t + 1)
                if t < 2:
                    a.activation(hb[:, t, 1, :], h2rows[t], ACT.Copy).then_inc(part2, 1)
                else:
                    link(a.activation(hb_s[32:64, :], h2rows[t][0:32, :], ACT.Copy))
                    a.activation(hb_mid, h2rows[t][0:32, :], ACT.Copy).then_inc(part2, 1)
            for t in range(3):
                n = TS[t]
                eng.wait_ge(top_done, t + 1)
                a.activation(gate[0:n, t, :], lg[0:n, t, :], ACT.Exp, bias=rs[0:n, t:t + 1]).then_inc(gexp_done, 1)
            for t in range(3):
                n = TS[t]
                eng.wait_ge(res2, t + 1)
                third = hb[0:n, t, 2, :] if t < 2 else hb_s[64:96, :]
                a.activation(third, h2rows[t][0:n, :], ACT.Copy).then_inc(part3, 1)

            eng.wait_ge(cum_ready, 1)
            for name in ("xT_a", "xT_b", "sig", "gT_copied", "aT_a", "aT_b"):
                eng.sem_inc(m[name], 1)

            def moe(p, lo, hi):
                with eng.Fori(lo, hi) as n:
                    n1 = eng.snap(n + 1)
                    n2 = eng.snap(n + 2)
                    eng.wait_ge(m["gath_a"], n2)
                    eng.wait_ge(m["L"], n1)
                    a.activation(xT[:, 0:256], bank[0][:, 0:256], ACT.Copy).then_inc(m["xT_a"], 1)
                    eng.wait_ge(m["gath_b"], n2)
                    a.activation(xT[:, 256:512], bank[2][:, 0:256], ACT.Copy).then_inc(m["xT_b"], 1)
                    eng.wait_ge(m["glu"], n2)
                    eng.wait_ge(m["act"], n1)
                    a.activation(gsig, glu, ACT.Sigmoid, scale=SW_ALPHA).then_inc(m["sig"], 1)
                    eng.wait_ge(m["gT"], n2)
                    a.activation(gpickT[:, :], bank[5][:, 0:NTOK], ACT.Copy).then_inc(m["gT_copied"], 1)
                    eng.wait_ge(m["T_a"], n2)
                    eng.wait_ge(m["S2"], n1)
                    a.activation(aT[:, 0:256], bank[3][:, 0:256], ACT.Copy).then_inc(m["aT_a"], 1)
                    eng.wait_ge(m["T_b"], n2)
                    a.activation(aT[:, 256:512], bank[1][:, 0:256], ACT.Copy).then_inc(m["aT_b"], 1)
                    eng.wait_ge(m["S2"], n2)
                    a.activation(outb, bank[4][:, :], ACT.Copy).then_inc(m["out"], 1)

            with eng.Fori(0, NE // 2) as i:
                for p in range(2):
                    moe(p, *block_range(eng, i, p))
            for t in range(3):
                n = TS[t]
                eng.wait_ge(fin_var, t + 1)
                a.activation(rstd[0:n, :], bnmv[0:n, 1:2], ACT.Sqrt).then_inc(fin_std, 1)

        @block.vector
        def _(dve):
            v = nc.vector
            count = [0]

            def link(ins):
                count[0] += 1
                ins.then_inc(dve_chain, 1)
                dve.wait_ge(dve_chain, count[0])

            v.memset(modr[:, :, :], 0.0)
            link(v.memset(cstat[:, :, :], 1.0))
            link(v.memset(rank[:, :, :], -1.0))
            link(v.memset(gate[:, :, :], 0.0))
            link(v.memset(maskf[:, :, :], 0.0))
            link(v.memset(cumf[:, :], 0.0))
            dve.wait_ge(csig_done, 1)
            v.tensor_tensor(scT[:, :, :].rearrange("p k g -> p g k"), cT[:, :, :], csig[:, :, :], ALU.mult).then_inc(scT_done, 1)

            def used(j):
                dve.wait_ge(tr_done, j + 1)
                return bank[2 + j % 2]

            ps = used(J_CS)
            pv = ps[:, 0:128].rearrange("p (c w) -> p c w", c=2)
            link(v.tensor_copy(cwT[:, :, 0:CONV_W], pv[:, :, 0:CONV_W]))
            v.tensor_copy(uext[:, :, U_S:U_S + PADW], pv[:, :, 32:32 + PADW]).then_inc(tr_used, 1)
            ps = used(J_KA)
            v.tensor_copy(kT_s[:, :, 0:PAST], ps[:, :].rearrange("p (j k) -> p j k", j=2)).then_inc(tr_used, 1)
            ps = used(J_KB)
            v.tensor_copy(kbT_s[:, 0:BCACHE], ps[:, 0:BCACHE]).then_inc(tr_used, 1)

            def add_mod(pair):
                dve.wait_ge(ada_done, 2 * pair + 2)
                dve.wait_ge(ld_bada[pair % 2], 32 * (pair // 2 + 1))
                if pair >= 4:
                    dve.wait_ge(st_mod[pair % 2], 32)
                elif pair >= 2:
                    dve.wait_ge(tr_done, J_M + 1)
                one = 1.0 if pair in (1, 4) else 0.0
                for j in range(2):
                    r = slice(32 * j, 32 * j + 2)
                    ins = v.scalar_tensor_tensor(out=modr[r, pair % 2, :], in0=bank[pair % 2][r, :], scalar=one,
                                                 in1=bada[r, pair % 2, :], op0=ALU.add, op1=ALU.add)
                    if j == 0:
                        link(ins)
                ins.then_inc(mod_ready, 1)

            add_mod(0)
            add_mod(1)
            pv = used(J_M)[:, 0:272].rearrange("p (a q r) -> p a q r", a=2, q=4)
            for j in range(2):
                for g in range(2):
                    ins = v.tensor_copy(modc[:, :, g, 4 * j:4 * j + 4], pv[:, :, :, 32 * j + g])
                    if (j, g) != (1, 1):
                        link(ins)
            ins.then_inc(tr_used, 1)
            dve.wait_ge(tr_used, J_M + 1)
            dve.wait_ge(ld["ext"], 32)
            for t in range(3):
                for j in range(2):
                    ps = used(J_H + 2 * t + j)
                    for q in range(4):
                        k = 4 * j + q
                        ins = v.tensor_scalar(hT[:, k, T0[t]:T0[t] + TS[t]], ps[:, P * q:P * q + TS[t]],
                                              modc[:, 1, GROUP[t], k:k + 1], modc[:, 0, GROUP[t], k:k + 1], ALU.mult, ALU.add)
                        if q < 3:
                            link(ins)
                    ins.then_inc(tr_used, 1)
            dve.wait_ge(masks_done, 1)
            dve.wait_ge(ld["cb"], 16)
            for c in range(2):
                dve.wait_ge(proj_used, 2 * c + 2)
                link(v.tensor_tensor(uext[:, c, PADW:U_S], uext[:, c, PADW:U_S], yconv[:, c, 0:SEQ], ALU.mult))
                link(v.tensor_tensor(uext[:, c, U_S + PADW:U_LEN], uext[:, c, U_S + PADW:U_LEN], yconv[:, c, SEQ:NTOK], ALU.mult))
            dve.sem_inc(u_gated, 1)
            for c in range(2):
                link(v.tensor_scalar(yconv[:, c, :], uext[:, c, 0:Y_LEN], cwT[:, c, 0:1], cbc[:, c:c + 1], ALU.mult, ALU.add))
                for w in range(1, CONV_W):
                    link(v.scalar_tensor_tensor(out=yconv[:, c, :], in0=uext[:, c, w:w + Y_LEN], scalar=cwT[:, c, w:w + 1],
                                                in1=yconv[:, c, :], op0=ALU.mult, op1=ALU.add))
            dve.sem_inc(conv_done, 1)
            dve.wait_ge(ld["cln"], 32)
            psy = [bank[2 + J_Y % 2][:, 0:256], bank[2 + J_Y % 2][:, 256:512], bank[2 + (J_Y + 1) % 2][:, 0:256]]
            for t in range(3):
                n = TS[t]
                used(J_Y + (t == 2))
                link(v.bn_stats(bnst[0:n, 0, :], psy[t][0:n, :]))
                link(v.bn_aggr(cstat[0:n, t, :], bnst[0:n, 0, :]))
            v.tensor_scalar(cstat[:, :, 1], cstat[:, :, 1], EPS, None, ALU.add).then_inc(conv_var, 1)
            dve.wait_ge(conv_std, 1)
            link(v.reciprocal(cstd[:, :], cstd[:, :]))
            for t in range(3):
                n = TS[t]
                ins = v.tensor_scalar(zrow[0:n, t, :], psy[t][0:n, :], cstat[0:n, t, 0:1], cstd[0:n, t:t + 1],
                                      ALU.subtract, ALU.mult)
                if t == 0:
                    link(ins)
                else:
                    ins.then_inc(tr_used, 1)
                    dve.wait_ge(tr_used, J_Y + t)
            for t in range(3):
                n = TS[t]
                link(v.tensor_tensor(zrow[0:n, t, :], zrow[0:n, t, :], clg[0:n, :], ALU.mult))
                ins = v.tensor_tensor(zrow[0:n, t, :], zrow[0:n, t, :], clb[0:n, :], ALU.add)
                if t < 2:
                    link(ins)
            ins.then_inc(conv_z, 1)
            for t in range(3):
                ps = used(J_KT + t)
                v.tensor_copy(ktok[0:TS[t], t, :], ps[0:TS[t], 0:384]).then_inc(tr_used, 1)
                dve.wait_ge(tr_used, J_KT + t + 1)
                dve.sem_inc(kt_ready, 1)
            ps = used(J_U)
            link(v.tensor_copy(ust, ps[0:PADW, :].rearrange("p (g c) -> p g c", g=2)))
            dve.sem_inc(ust_ready, 1)
            dve.sem_inc(tr_used, 1)
            for t in range(3):
                n = TS[t]
                dve.wait_ge(conv_sig, t + 1)
                v.tensor_tensor(zrow[0:n, t, :], zrow[0:n, t, :], zsig[0:n, t, :], ALU.mult).then_inc(conv_out, 1)
            ps = used(J_Z)
            pv = ps[:, :].rearrange("p (t c n) -> p t c n", t=2, c=2)
            link(v.tensor_copy(hT[:, 6:8, 0:P], pv[:, 0]))
            v.tensor_copy(hT[:, 6:8, P:2 * P], pv[:, 1]).then_inc(tr_used, 1)
            ps = used(J_Z + 1)
            v.tensor_copy(hT[:, 6:8, SEQ:NTOK], ps[:, 0:64].rearrange("p (c n) -> p c n", c=2)).then_inc(tr_used, 1)
            link(v.tensor_copy(kT_s[:, :, PAST:SA_K], qkT[:, 2:4, SEQ:NTOK]))
            v.tensor_copy(kbT_s[:, BCACHE:SB_K], qkT[:, 8, SEQ:NTOK]).then_inc(keys_ready, 1)
            dve.wait_ge(ld["sinks"], 9 * 16)
            link(v.tensor_scalar(nsink[:, :], nsink[:, :], -1.0, None, ALU.mult))
            link(v.tensor_scalar(nsink_s[:, :], nsink_s[:, :], -1.0, None, ALU.mult))

            def maxima(s):
                kind, t, j = ATT[s]
                nk = keys_of(kind, t)
                nh = 1 if t == 2 else 2
                dve.wait_ge(log_done, s + 1)
                if s >= 1:
                    dve.wait_ge(negm_done, s)
                for h in range(nh):
                    link(v.tensor_reduce(mx[:, h:h + 1], logit_bank(s, h)[:, 0:nk], AX_X, ALU.max))
                st = stat[:, s % 2, 0:nh]
                if kind in ("A", "SA"):
                    v.tensor_scalar(st, mx[:, 0:nh], -1.0, None, ALU.mult).then_inc(negm_done, 1)
                else:
                    ns = nsink[:, :].rearrange("p (n i) -> p i n", n=2)[:, j, :] if kind == "B" else nsink_s[:, j:j + 1]
                    link(v.scalar_tensor_tensor(out=st, in0=mx[:, 0:nh], scalar=-1.0, in1=ns, op0=ALU.mult, op1=ALU.min))
                    v.tensor_tensor(dsink[:, s % 2, 0:nh], st, ns, ALU.subtract).then_inc(negm_done, 1)

            def normalise(s):
                kind, t, j = ATT[s]
                nk = keys_of(kind, t)
                nh = 1 if t == 2 else 2
                dve.wait_ge(exp_done, exps_through(s))
                if s >= 1:
                    dve.wait_ge(prob_done, probs_through(s - 1))
                pr = prob[:, s % 2, :, :] if nh == 2 else prob[:, s % 2, :, :].rearrange("p h k -> p (h k)").unsqueeze(1)
                es = esum[:, s % 2, 0:nh]
                if kind in ("B", "SB"):
                    link(v.tensor_tensor(es, es, esink[:, s % 2, 0:nh], ALU.add))
                link(v.reciprocal(rinv[:, 0:nh], es))
                for h in range(nh):
                    v.tensor_scalar(pr[:, h, 0:nk], pr[:, h, 0:nk], rinv[:, h:h + 1], None, ALU.mult).then_inc(prob_done, 1)

            def copy_o(s):
                kind, t, j = ATT[s]
                dve.wait_ge(o_done, s + 1)
                if t < 2:
                    ins = v.tensor_copy(hT[:, (0 if kind == "A" else 2) + j, T0[t]:T0[t] + P], bank[7][:, 0:P])
                elif kind == "SA":
                    ins = v.tensor_copy(hT[:, 0:2, SEQ:NTOK], bank[7][:, 0:64].rearrange("p (j q) -> p j q", j=2))
                else:
                    r = slice(64 * j, 64 * j + 64)
                    ins = v.tensor_copy(hT[r, 2:6, SEQ:NTOK], bank[7][r, 0:P].rearrange("p (i q) -> p i q", i=4))
                ins.then_inc(o_copied, 1)

            maxima(0)
            for s in range(NATT):
                if s + 1 < NATT:
                    maxima(s + 1)
                normalise(s)
                if s >= 1:
                    copy_o(s - 1)
                if s in (1, 3, 5, 7):
                    add_mod(2 + s // 2)
            copy_o(NATT - 1)

            def norm_rows(rows, gain, shift, t, var, std, n):
                for j in range(2):
                    link(v.bn_stats(bnst[0:n, j, :], rows[:, 512 * j:512 * (j + 1)]))
                link(v.bn_aggr(bnmv[0:n, :], bnst[0:n, :, :]))
                link(v.tensor_scalar(bnmv[0:n, 1:2], bnmv[0:n, 1:2], EPS, None, ALU.add))
                dve.sem_inc(var, 1)
                dve.wait_ge(std, t + 1)
                link(v.reciprocal(rstd[0:n, :], rstd[0:n, :]))
                link(v.tensor_scalar(rows, rows, bnmv[0:n, 0:1], rstd[0:n, :], ALU.subtract, ALU.mult))
                link(v.tensor_tensor(rows, rows, gain[0:n, :], ALU.mult))
                return v.tensor_tensor(rows, rows, shift[0:n, :], ALU.add)

            dve.wait_ge(ld["brow"], 8 * 16)
            for t in range(3):
                n, g = TS[t], GROUP[t]
                rows = XY[0:n, t, :]
                dve.wait_ge(op_done, t + 1)
                h2row = h2rows[t]
                for j in range(2):
                    ps = bank[4 + 2 * t + j][:, :] if t < 2 else bank[0][32 * j:32 * j + 32, :]
                    link(v.tensor_tensor(h2row[0:n, 512 * j:512 * (j + 1)], ps[0:n, :] if t < 2 else ps,
                                         g1b[0:n, g, 512 * j:512 * (j + 1)], ALU.mult))
                link(v.scalar_tensor_tensor(out=rows, in0=rows, scalar=ALPHA, in1=h2row[0:n, :], op0=ALU.mult, op1=ALU.add))
                norm_rows(rows, lng, lnb, t, ln_var, ln_std, n).then_inc(x1_ready, 1)
                dve.wait_ge(x1_ready, t + 1)
                link(v.tensor_tensor(h2row[0:n, :], rows, sc2b[0:n, g, :], ALU.mult))
                v.tensor_tensor(h2row[0:n, :], h2row[0:n, :], sh2b[0:n, g, :], ALU.add).then_inc(h2_ready, 1)

            dve.wait_ge(ld["wr"], 32)
            for t in range(3):
                n = TS[t]
                dve.wait_ge(lg_done, t + 1)
                L = lg[0:n, t, :]
                link(v.tensor_tensor(L, bank[(1, 6, 7)[t]][0:n, 0:NE], brb[0:n, :], ALU.add))
                link(v.max(top8[0:n, :], L))
                v.tensor_scalar(rs[0:n, t:t + 1], top8[0:n, 0:1], -1.0, None, ALU.mult).then_inc(top_done, 1)
                above, tied, order, tmp = (rt[0:n, j, :] for j in range(4))
                link(v.tensor_scalar(above, L, top8[0:n, 3:4], None, ALU.is_gt))
                link(v.tensor_scalar(tied, L, top8[0:n, 3:4], None, ALU.is_equal))
                link(v.tensor_reduce(rs[0:n, 3:4], above, AX_X, ALU.add))
                link(v.tensor_tensor_scan(order, tied, tied, 0.0, ALU.add, ALU.max))
                link(v.tensor_scalar(order, order, rs[0:n, 3:4], float(TOPK), ALU.add, ALU.is_le))
                link(v.tensor_tensor(tied, tied, order, ALU.mult))
                link(v.tensor_tensor(maskf[0:n, t, :], above, tied, ALU.add))
                v.tensor_copy(maskb[0:n, t, :], maskf[0:n, t, :]).then_inc(mask_done, 1)
                dve.wait_ge(gexp_done, t + 1)
                link(v.tensor_tensor(gate[0:n, t, :], gate[0:n, t, :], maskf[0:n, t, :], ALU.mult))
                link(v.tensor_reduce(rs[0:n, 3:4], gate[0:n, t, :], AX_X, ALU.add))
                link(v.reciprocal(rs[0:n, 3:4], rs[0:n, 3:4]))
                link(v.tensor_scalar(gate[0:n, t, :], gate[0:n, t, :], rs[0:n, 3:4], None, ALU.mult))
            dve.wait_ge(rank_done, 1)
            for t in range(3):
                n = TS[t]
                link(v.scalar_tensor_tensor(out=rank[0:n, t, :], in0=bank[1][0:n, 128 + NE * t:128 + NE * (t + 1)], scalar=1.0,
                                            in1=maskf[0:n, t, :], op0=ALU.add, op1=ALU.mult))
                link(v.tensor_scalar(rank[0:n, t, :], rank[0:n, t, :], -1.0, None, ALU.add))
            for j in (1, 2):
                link(v.tensor_copy(rank[32 * j:32 * j + 32, 2, :], rank[0:32, 2, :]))
            link(v.tensor_copy(cnt[0:1, 0, :], bank[1][0:1, 256:256 + NE]))
            link(v.tensor_scalar(cnt[0:1, 1, :], cnt[0:1, 0, :], float(SLOTS), 1.0, ALU.is_gt, ALU.add))
            for j in range(2, 5):
                link(v.scalar_tensor_tensor(out=cnt[0:1, 1, :], in0=cnt[0:1, 0, :], scalar=float(SLOTS * j),
                                            in1=cnt[0:1, 1, :], op0=ALU.is_gt, op1=ALU.add))
            link(v.tensor_tensor_scan(cumf[0:1, 3:NE + 3], cnt[0:1, 1, :], cnt[0:1, 1, :], 0.0, ALU.add, ALU.max))
            dve.wait_ge(ld["x1s"], 48)
            link(v.memset(XY[:, :, :], 0.0))
            dve.wait_ge(part3, 3)
            link(v.memset(outb, 0.0))
            link(v.memset(gpickT[:, :], 0.0))
            v.tensor_copy(cum[:, :], cumf[:, :]).then_inc(cum_ready, 1)
            dve.wait_ge(cum_ready, 1)
            for name in ("pick", "glu", "gs", "y01", "lin_a", "lin", "act_a", "act", "y2"):
                dve.sem_inc(m[name], 1)
            dve.sem_inc(m["out"], 1)

            def add_y(t, banks, sem_, val_):
                for h in range(2):
                    ins = v.tensor_tensor(XY[0:TS[t], t, 512 * h:512 * (h + 1)], bank[banks[h]][0:TS[t], :],
                                          XY[0:TS[t], t, 512 * h:512 * (h + 1)], ALU.add)
                return ins

            def moe(p, e, lo, hi):
                free = dve.snap(dve.value_load(cum[0:1, bass.ds(e + 1, 1)], min_val=0, max_val=160) + 1,
                                min_val=1, max_val=161)
                picked = dve.snap(lo + 1)
                e1 = dve.snap(e + 1)
                dve.wait_ge(m["S2"], free)
                v.tensor_scalar(sel[:, p, :], eye3[:, bass.ds(e, 1)].to_broadcast([96, SLOTS]), 1.0, None, ALU.mult)\
                 .then_inc(sel_ready, 1)
                dve.wait_ge(m["pick"], picked)
                v.tensor_scalar(rkc[:, :, :], rank[:, :, bass.ds(e, 1)], 1.0, None, ALU.mult).then_inc(cur_ready, 1)
                v.tensor_scalar(gtc[:, :, :], gate[:, :, bass.ds(e, 1)], 1.0, None, ALU.mult).then_inc(cur_ready, 1)
                e2 = dve.snap(2 * e1)
                with dve.Fori(lo, hi) as n:
                    n1 = dve.snap(n + 1)
                    n2 = dve.snap(n + 2)
                    at = nc.s_assert_within(dve.snap((n - lo) * (2 * SLOTS)), 0, 4 * 2 * SLOTS, skip_runtime_bounds_check_because="an expert has at most five blocks")
                    dve.wait_ge(cur_ready, e2)
                    dve.wait_ge(m["gath_b"], n1)
                    dve.wait_ge(m["gT"], n1)
                    for t in range(3):
                        r = TS[t] if t < 2 else 96
                        v.tensor_scalar(pick[0:r, t, :], iota[0:r, bass.ds(at, SLOTS)], rkc[0:r, t, :], None, ALU.is_equal)
                    for t in range(3):
                        ins = v.tensor_scalar(gpick[0:TS[t], t, :], iota[0:TS[t], bass.ds(at, 2 * SLOTS)], rkc[0:TS[t], t, :],
                                              gtc[0:TS[t], t, :], ALU.is_equal, ALU.mult)
                    ins.then_inc(m["pick"], 1)
                    dve.wait_ge(m["G"], n2)
                    dve.wait_ge(m["gs"], n1)
                    v.tensor_scalar(glu, bank[1][:, :], LIMIT, None, ALU.min).then_inc(m["glu"], 1)
                    dve.wait_ge(m["sig"], n2)
                    v.tensor_tensor(gsig, gsig, glu, ALU.mult).then_inc(m["gs"], 1)
                    dve.wait_ge(m["c01"], n2)
                    dve.wait_ge(m["y01"], n1)
                    add_y(0, (3, 4), None, None)
                    add_y(1, (5, 0), None, None).then_inc(m["y01"], 1)
                    dve.wait_ge(m["L"], n2)
                    dve.wait_ge(m["act"], n1)
                    v.tensor_scalar(lin[:, 0:256], bank[2][:, 0:256], LIMIT, -LIMIT, ALU.min, ALU.max).then_inc(m["lin_a"], 1)
                    v.tensor_scalar(lin[:, 256:512], bank[2][:, 256:512], LIMIT, -LIMIT, ALU.min, ALU.max).then_inc(m["lin"], 1)
                    dve.wait_ge(m["lin_a"], n2)
                    dve.wait_ge(m["T_b"], n1)
                    v.scalar_tensor_tensor(out=act[:, 0:256], in0=lin[:, 0:256], scalar=1.0, in1=gsig[:, 0:256],
                                           op0=ALU.add, op1=ALU.mult).then_inc(m["act_a"], 1)
                    dve.wait_ge(m["lin"], n2)
                    v.scalar_tensor_tensor(out=act[:, 256:512], in0=lin[:, 256:512], scalar=1.0, in1=gsig[:, 256:512],
                                           op0=ALU.add, op1=ALU.mult).then_inc(m["act"], 1)
                    dve.wait_ge(m["c2"], n2)
                    dve.wait_ge(m["y2"], n1)
                    add_y(2, (6, 7), None, None).then_inc(m["y2"], 1)

            with dve.Fori(0, NE // 2) as i:
                for p in range(2):
                    moe(p, dve.snap(2 * i + p, min_val=0, max_val=NE - 1), *block_range(dve, i, p))

            total = dve.snap(dve.value_load(cum[0:1, NE + 2:NE + 3], min_val=32, max_val=160) + 1, min_val=33, max_val=161)
            dve.wait_ge(m["y01"], total)
            dve.wait_ge(m["y2"], total)
            for t, banks in enumerate(((3, 4), (5, 0), (6, 7))):
                dve.wait_ge(fin_c, t + 1)
                ins = add_y(t, banks, None, None)
                ins.then_inc(fin_y, 1)

            dve.wait_ge(ld["final"], 7 * 16)
            for t in range(3):
                n, g = TS[t], GROUP[t]
                rows = x1_fin[0:n, t, :]
                dve.wait_ge(fin_y, t + 1)
                link(v.tensor_tensor(XY[0:n, t, :], XY[0:n, t, :], g2b[0:n, g, :], ALU.mult))
                link(v.scalar_tensor_tensor(out=rows, in0=rows, scalar=ALPHA, in1=XY[0:n, t, :], op0=ALU.mult, op1=ALU.add))
                norm_rows(rows, lng2, lnb2, t, fin_var, fin_std, n).then_inc(fin_ready, 1)

        @block.tensor
        def _(pe):
            mm = nc.tensor.matmul

            def job(j):
                if j >= 2:
                    pe.wait_ge(tr_used, j - 1)
                return bank[2 + j % 2]

            pe.wait_ge(consts_done, 2)
            pe.wait_ge(ld["cs"], 32)
            ps = job(J_CS)
            for c in range(2):
                ins = nc.tensor.transpose(ps[:, 64 * c:64 * c + 64], cs[:, P * c:P * (c + 1)], ident[0:64, 0:64])
            ins.then_inc(tr_done, 1)
            pe.wait_ge(ld["ka"], 16)
            ps = job(J_KA)
            for j in range(2):
                for t in range(2):
                    ins = nc.tensor.transpose(ps[:, PAST * j + P * t:PAST * j + P * (t + 1)], ka_c[:, t, P * j:P * (j + 1)], ident[:, :])
            ins.then_inc(tr_done, 1)
            pe.wait_ge(ld["kb"], 16)
            ps = job(J_KB)
            nc.tensor.transpose(ps[:, 0:P], kb_c, ident[:, :]).then_inc(tr_done, 1)

            def ada(u):
                pair, half = divmod(u, 2)
                pe.wait_ge(ld_ada[u % 2], 16 * (u // 2 + 1))
                if half == 0 and pair >= 2:
                    pe.wait_ge(mod_ready, pair - 1)
                for q in range(4):
                    k = 4 * half + q
                    for j in range(2):
                        ins = mm(bank[pair % 2][32 * j:32 * j + 2, :], scT[:, k, :], ring[:, u % 2, q, 512 * j:512 * (j + 1)],
                                 start=(k == 0), stop=(k == DK - 1))
                ins.then_inc(ada_done, 1)

            pe.wait_ge(scT_done, 1)
            for u in range(4):
                ada(u)
            pe.wait_ge(mod_ready, 2)
            ps = job(J_M)
            for pair in range(2):
                for q in range(4):
                    at = 34 * (4 * pair + q)
                    ins = nc.tensor.transpose(ps[:, at:at + 34], modr[:, pair, P * q:P * (q + 1)], ident[0:34, 0:34])
            ins.then_inc(tr_done, 1)
            pe.wait_ge(ld["x"], 32)
            for t in range(3):
                for j in range(2):
                    ps = job(J_H + 2 * t + j)
                    for q in range(4):
                        k = 4 * j + q
                        ins = nc.tensor.transpose(ps[:, P * q:P * q + TS[t]], XY[0:TS[t], t, P * k:P * (k + 1)], ident[0:TS[t], 0:TS[t]])
                    ins.then_inc(tr_done, 1)

            win = w1v[0]
            pe.wait_ge(tr_used, J_H + 6)
            for n, name in enumerate(PROJ + ["v0", "v1", "v2"]):
                ps = bank[4 + n % 2]
                if name in ("gg0", "k0", "qb0", "kb"):
                    piece = PIECE[name[:2] if name in ("qb0", "kb") else name[0]]
                    pe.wait_ge(ld_win[piece], (16, 16, 16 * BH, 32)[piece])
                if n >= 2:
                    pe.wait_ge(proj_used, n - 1)
                if name[0] == "v":
                    t = int(name[1])
                    for at, a, b in ((0, W_VA, W_QB), (256, W_VB, W_G)):
                        for k in range(DK):
                            ins = mm(ps[0:TS[t], at:at + b - a], hT[:, k, T0[t]:T0[t] + TS[t]], win[:, k, a:b],
                                     start=(k == 0), stop=(k == DK - 1))
                else:
                    for k in range(DK):
                        if name[:2] == "gg":
                            w = win[:, k, W_G + 256 + P * int(name[2]):W_G + 256 + P * int(name[2]) + P]
                        elif name[:2] == "ga":
                            w = win[:, k, W_G + P * int(name[2]):W_G + P * int(name[2]) + P]
                        elif name == "kb":
                            w = win[:, k, W_KB:W_KB + P]
                        elif name[:2] == "qb":
                            w = win[:, k, W_QB + P * int(name[2]):W_QB + P * int(name[2]) + P]
                        else:
                            at = (W_K if name[0] == "k" else 0) + P * int(name[1])
                            w = win[:, k, at:at + P]
                        ins = mm(ps[:, 0:NTOK], w, hT[:, k, :], start=(k == 0), stop=(k == DK - 1))
                ins.then_inc(proj_done, 1)

            pe.wait_ge(conv_done, 1)
            ps = job(J_Y)
            for t in range(2):
                for c in range(2):
                    ins = nc.tensor.transpose(ps[:, 256 * t + P * c:256 * t + P * (c + 1)], yconv[:, c, P * t:P * (t + 1)], ident[:, :])
            ins.then_inc(tr_done, 1)
            ps = job(J_Y + 1)
            for c in range(2):
                ins = nc.tensor.transpose(ps[0:32, P * c:P * (c + 1)], yconv[:, c, U_S:U_S + DEC], ident[:, :])
            ins.then_inc(tr_done, 1)
            pe.wait_ge(proj_used, NPROJ)
            for t in range(3):
                ps = job(J_KT + t)
                for j, at in enumerate((2, 3, 8)):
                    ins = nc.tensor.transpose(ps[0:TS[t], P * j:P * (j + 1)], qkT[:, at, T0[t]:T0[t] + TS[t]], ident[:, :])
                ins.then_inc(tr_done, 1)
            ps = job(J_U)
            for g, at in enumerate((U_S - PADW, U_LEN - PADW)):
                for c in range(2):
                    ins = nc.tensor.transpose(ps[0:PADW, 256 * g + P * c:256 * g + P * (c + 1)], uext[:, c, at:at + PADW], ident[:, :])
            ins.then_inc(tr_done, 1)
            pe.wait_ge(conv_out, 3)
            ps = job(J_Z)
            for t in range(2):
                for c in range(2):
                    ins = nc.tensor.transpose(ps[:, 256 * t + P * c:256 * t + P * (c + 1)], zrow[:, t, P * c:P * (c + 1)], ident[:, :])
            ins.then_inc(tr_done, 1)
            ps = job(J_Z + 1)
            for c in range(2):
                ins = nc.tensor.transpose(ps[:, 32 * c:32 * c + 32], zrow[0:32, 2, P * c:P * (c + 1)], ident[0:32, 0:32])
            ins.then_inc(tr_done, 1)

            def logits(s):
                kind, t, j = ATT[s]
                nk = keys_of(kind, t)
                if s >= 2:
                    pe.wait_ge(exp_done, exps_through(s - 2))
                ps = logit_bank(s, 0)
                if t < 2:
                    for h in range(2):
                        out = logit_bank(s, h)[:, 0:nk]
                        head = 2 * j + h if kind == "A" else 4 * h + j
                        bias = (bias_a if kind == "A" else bias_b)[:, head, 256 - nk:256]
                        mm(out, anti[:, :], bias, start=True, stop=False)
                        r = slice(64 * h, 64 * h + 64)
                        q, k = (j, 2 + j) if kind == "A" else (4 + j, 8)
                        ins = mm(out, qkT[r, q, P * t:P * (t + 1)], qkT[r, k, 0:nk], start=False, stop=True)
                else:
                    mm(ps[:, 0:nk], anti32[:, :], bias_sa if kind == "SA" else bias_sb[:, j, :], start=True, stop=False,
                       skip_group_check=True)
                    for h in range(4):
                        if kind == "SA":
                            r = slice(64 * (h % 2), 64 * (h % 2) + 64)
                            q, keys = qkT[r, h // 2, SEQ:NTOK], kT_s[r, h // 2, :]
                        else:
                            r = slice(64 * j, 64 * j + 64)
                            q, keys = qkT[r, 4 + h, SEQ:NTOK], kbT_s[r, :]
                        ins = mm(ps[32 * h:32 * h + 32, 0:nk], q, keys, start=False, stop=True, skip_group_check=True)
                ins.then_inc(log_done, 1)

            def transpose_p(s):
                kind, t, j = ATT[s]
                nk = keys_of(kind, t)
                pe.wait_ge(prob_done, probs_through(s))
                if s >= 1:
                    pe.wait_ge(pT_copied, s)
                pr = prob[:, s % 2, :, :]
                nh = 1 if t == 2 else 2
                if nh == 1:
                    pr = pr.rearrange("p h k -> p (h k)").unsqueeze(1)
                at = 0
                for h in range(nh):
                    for k in range(0, nk, P):
                        w = min(P, nk - k)
                        ins = nc.tensor.transpose(bank[6][0:w, at:at + P], pr[:, h, k:k + w], ident[:, :])
                        at += P
                ins.then_inc(pT_done, 1)

            def values(s):
                kind, t, j = ATT[s]
                nk = keys_of(kind, t)
                nt = -(-nk // P)
                pe.wait_ge(pT_copied, s + 1)
                if s >= 1:
                    pe.wait_ge(o_copied, s)
                ps = bank[7]
                if t < 2:
                    for h in range(2):
                        c = 64 * (2 * j + h) if kind == "A" else 256 + 64 * h
                        for k in range(nt):
                            ins = mm(ps[64 * h:64 * h + 64, 0:P], vtok[:, k, c:c + 64], pT[:, P * (nt * h + k):P * (nt * h + k + 1)],
                                     start=(k == 0), stop=(k == nt - 1))
                elif kind == "SA":
                    for h in range(4):
                        for k in range(3):
                            vals = va_c[:, k, 64 * h:64 * h + 64] if k < 2 else vtok[0:32, 2, 64 * h:64 * h + 64]
                            w = P if k < 2 else 32
                            ins = mm(ps[64 * (h % 2):64 * (h % 2) + 64, 32 * (h // 2):32 * (h // 2) + 32], vals,
                                     pT[0:w, P * k + 32 * h:P * k + 32 * h + 32], start=(k == 0), stop=(k == 2))
                else:
                    for k in range(2):
                        vals = vb_c[:, 64 * j:64 * j + 64] if k == 0 else vtok[0:32, 2, 256 + 64 * j:256 + 64 * j + 64]
                        w = P if k == 0 else 32
                        ins = mm(ps[64 * j:64 * j + 64, 0:P], vals, pT[0:w, P * k:P * (k + 1)], start=(k == 0), stop=(k == 1))
                ins.then_inc(o_done, 1)

            pe.wait_ge(ld["toep"], 10 * 16)
            pe.wait_ge(masks_done, 4)
            pe.wait_ge(keys_ready, 1)
            pe.wait_ge(ld["v"], 32)
            logits(0)
            for s in range(NATT):
                if s + 1 < NATT:
                    logits(s + 1)
                if s < 8:
                    ada(4 + s)
                transpose_p(s)
                values(s)

            pe.wait_ge(ld["wout"], 6 * 16)
            pe.wait_ge(o_copied, NATT)
            pe.wait_ge(tr_used, J_Z + 2)
            pe.wait_ge(mod_ready, 6)
            for t in range(2):
                for j in range(2):
                    for k in range(DK):
                        ins = mm(bank[4 + 2 * t + j][:, :], hT[:, k, P * t:P * (t + 1)], w2v[:, k, 512 * j:512 * (j + 1)],
                                 start=(k == 0), stop=(k == DK - 1))
                ins.then_inc(op_done, 1)
            for k in range(DK):
                for j in range(2):
                    ins = mm(bank[0][32 * j:32 * j + 32, :], hT[:, k, SEQ:NTOK], w2v[:, k, 512 * j:512 * (j + 1)],
                             start=(k == 0), stop=(k == DK - 1))
            ins.then_inc(op_done, 1)

            pe.wait_ge(ld["wr"], 32)
            for t in range(3):
                n = TS[t]
                pe.wait_ge(h2_ready, t + 1)
                for j in range(2):
                    if t >= 1:
                        pe.wait_ge(h2T_copied, 2 * t + j - 1)
                    for q in range(4):
                        k = 4 * j + q
                        ins = nc.tensor.transpose(bank[2 + j][:, P * q:P * q + n], h2rows[t][0:n, P * k:P * (k + 1)], ident[0:n, 0:n])
                    ins.then_inc(h2T_done, 1)
                pe.wait_ge(h2T_copied, 2 * t + 2)
                for k in range(DK):
                    ins = mm(bank[(1, 6, 7)[t]][0:n, 0:NE], hT[:, k, T0[t]:T0[t] + n], wr[:, k, :], start=(k == 0), stop=(k == DK - 1))
                ins.then_inc(lg_done, 1)
            pe.wait_ge(mask_done, 3)
            for t in range(3):
                n = TS[t]
                out = bank[1][0:n, 128 + NE * t:128 + NE * (t + 1)]
                for b in range(t):
                    mm(out, ones[:, 0:n], maskb[:, b, :], start=(b == 0), stop=False)
                mm(out, upper[0:n, 0:n], maskb[0:n, t, :], start=(t == 0), stop=True)
            for t in range(3):
                ins = mm(bank[1][0:1, 256:256 + NE], ones[0:TS[t], 0:1], maskb[0:TS[t], t, :], start=(t == 0), stop=(t == 2))
            ins.then_inc(rank_done, 1)

            pe.wait_ge(cum_ready, 1)
            pe.wait_ge(b3_done, 1)
            for name in ("gath_a", "gath_b", "G", "c01", "L", "c2", "gT", "T_a", "T_b", "S2"):
                pe.sem_inc(m[name], 1)
            tiles = ((0, (3, 4)), (1, (5, 0)), (2, (6, 7)))

            def combine(t, banks):
                for h in range(2):
                    ins = mm(bank[banks[h]][0:TS[t], :], gpickT[64 * h:64 * h + 64, T0[t]:T0[t] + TS[t]], outb[64 * h:64 * h + 64, :],
                             start=True, stop=True)
                return ins

            def moe(p, i, lo, hi):
                e1 = pe.snap(2 * i + (p + 1))
                w1 = pe.snap(32 * i + 32)
                w2 = pe.snap(64 * i + 32 * (p + 1))
                w1t, w2t = w1v[p], w2v
                with pe.Fori(lo, hi) as n:
                    n1 = pe.snap(n + 1)
                    n2 = pe.snap(n + 2)
                    pe.wait_ge(m["y01"], n1)
                    pe.wait_ge(m["pick"], n2)
                    for k in range(DK):
                        if k == 4:
                            pe.wait_ge(m["lin"], n1)
                        out = bank[0 if k < 4 else 2][:, SLOTS * (k % 4):SLOTS * (k % 4 + 1)]
                        for t in range(2):
                            for j in range(3):
                                mm(out, hb[:, t, j, P * k:P * (k + 1)], pick[:, t, :], start=(t == 0 and j == 0), stop=False)
                        ins = mm(out, hb_s[0:96, P * k:P * (k + 1)], pick[0:96, 2, :], start=False, stop=True)
                        if k == 3:
                            ins.then_inc(m["gath_a"], 1)
                    ins.then_inc(m["gath_b"], 1)

                    def up(bk, first, done):
                        for h in range(2):
                            mm(bank[bk][64 * h:64 * h + 64, :], sel[:, p, :], B3[:, first + 512 * h:first + 512 * (h + 1)],
                               start=True, stop=False)
                        for k in range(DK):
                            if bk == 1 and k == 0:
                                pe.wait_ge(m["xT_a"], n2)
                                pe.wait_ge(ld_glu[p], w1)
                            if bk == 2 and k == 0:
                                pe.wait_ge(ld_lin[p], w1)
                            if bk == 1 and k == 4:
                                pe.wait_ge(m["xT_b"], n2)
                            for h in range(2):
                                ins = mm(bank[bk][64 * h:64 * h + 64, :], xT[:, SLOTS * k:SLOTS * (k + 1)],
                                         w1t[:, k, first + 512 * h:first + 512 * (h + 1)], start=False, stop=(k == DK - 1))
                        ins.then_inc(m[done], 1)

                    pe.wait_ge(m["out"], n1)
                    pe.wait_ge(m["gT_copied"], n1)
                    pe.wait_ge(m["aT_b"], n1)
                    combine(*tiles[0])
                    pe.wait_ge(sel_ready, e1)
                    up(1, 0, "G")
                    pe.wait_ge(m["y2"], n1)
                    combine(*tiles[1]).then_inc(m["c01"], 1)
                    up(2, D, "L")
                    combine(*tiles[2]).then_inc(m["c2"], 1)
                    pe.wait_ge(m["y01"], n2)
                    for t in range(3):
                        ins = nc.tensor.transpose(bank[5][:, T0[t]:T0[t] + TS[t]], gpick[0:TS[t], t, :], ident[0:TS[t], 0:TS[t]])
                    ins.then_inc(m["gT"], 1)
                    for j in range(4):
                        if j % 2 == 0:
                            pe.wait_ge(m["act_a" if j == 0 else "act"], n2)
                        ins = nc.tensor.transpose(bank[3 if j < 2 else 1][:, P * (j % 2):P * (j % 2 + 1)], act[:, P * j:P * (j + 1)], ident[:, :])
                        if j == 1:
                            ins.then_inc(m["T_a"], 1)
                    ins.then_inc(m["T_b"], 1)
                    for h in range(2):
                        mm(bank[4][64 * h:64 * h + 64, :], sel[:, p, :], B3[:, 2 * D + 512 * h:2 * D + 512 * (h + 1)],
                           start=True, stop=False)
                    for j in range(4):
                        if j == 0:
                            pe.wait_ge(m["aT_a"], n2)
                            pe.wait_ge(ld_w2, w2)
                        if j == 2:
                            pe.wait_ge(m["aT_b"], n2)
                        for k in (j, 4 + j):
                            for h in range(2):
                                ins = mm(bank[4][64 * h:64 * h + 64, :], aT[:, P * j + SLOTS * (k // 4):P * j + SLOTS * (k // 4) + SLOTS],
                                         w2t[:, k, 512 * h:512 * (h + 1)], start=False, stop=(j == 3 and k == 7))
                    ins.then_inc(m["S2"], 1)

            with pe.Fori(0, NE // 2) as i:
                for p in range(2):
                    moe(p, i, *block_range(pe, i, p))
            total = pe.snap(pe.value_load(cum[0:1, NE + 2:NE + 3], min_val=32, max_val=160) + 1, min_val=33, max_val=161)
            pe.wait_ge(m["out"], total)
            pe.wait_ge(m["gT_copied"], total)
            pe.wait_ge(m["y2"], total)
            for t, banks in tiles:
                combine(t, banks).then_inc(fin_c, 1)


_OUTS = [(1, SEQ, D), (1, DEC, D), (1, 1, 256, AH, HD), (1, 1, 256, AH, HD), (1, 1, 128, 2, HD), (1, 1, 128, 2, HD),
         (1, 1, PADW, C_CH), (1, 1, 256, AH, HD), (1, 1, 256, AH, HD), (1, 1, 128, 2, HD), (1, 1, 128, 2, HD), (1, 1, PADW, C_CH)]


def kernel(x_prompt, x_sample, cache_a_k, cache_a_v, cache_b_k, cache_b_v, state_conv, c_prompt, c_sample, w_in, w_out,
           rel_bias_a, t5_bias, sinks, conv_w, conv_b, conv_ln_g, conv_ln_b, w_ada, b_ada, ln_g, ln_b, w_router, b_router,
           w_e_in, b_e_in, w_e_out, b_e_out):
    import numpy as _np
    import concourse.bacc as _bacc
    from concourse.bass_utils import run_bass_kernel_spmd as _run

    ins = dict(x_prompt=x_prompt, x_sample=x_sample, cache_a_k=cache_a_k, cache_a_v=cache_a_v, cache_b_k=cache_b_k,
               cache_b_v=cache_b_v, state_conv=state_conv, c_prompt=c_prompt, c_sample=c_sample, w_in=w_in, w_out=w_out,
               rel_bias_a=rel_bias_a, t5_bias=t5_bias, sinks=sinks, conv_w=conv_w, conv_b=conv_b, conv_ln_g=conv_ln_g,
               conv_ln_b=conv_ln_b, w_ada=w_ada, b_ada=b_ada, ln_g=ln_g, ln_b=ln_b, w_router=w_router, b_router=b_router,
               w_e_in=w_e_in, b_e_in=b_e_in, w_e_out=w_e_out, b_e_out=b_e_out)
    nc = _bacc.Bacc("TRN2", target_bir_lowering=False, num_devices=1, dynamic_dma_scratch_size=1024)
    arrays, args = {}, []
    for name, a in ins.items():
        a = _np.ascontiguousarray(a)
        arrays[f"in_{name}"] = a
        args.append(nc.dram_tensor(f"in_{name}", a.shape, mybir.dt.from_np(a.dtype), kind="ExternalInput").ap())
    for i, shape in enumerate(_OUTS):
        args.append(nc.dram_tensor(f"out_{i}", shape, F32, kind="ExternalOutput").ap())
    args.append(nc.dram_tensor("mod_rows", (2, 6 * D), F32, kind="Internal").ap())
    args.append(nc.dram_tensor("ext_rows", (AH + BH, EXT), F32, kind="Internal").ap())
    args.append(nc.dram_tensor("x1_rows", (NTOK, D), F32, kind="Internal").ap())
    hybrid_streaming_encoder_step(nc, *args)
    r = _run(nc, [arrays], core_ids=[0])
    return tuple(r.results[0][f"out_{i}"] for i in range(len(_OUTS)))
```
